# Optimizing a Trainium2 kernel written in Bass

```python
import jax, jax.numpy as jnp
from jax import lax
import numpy as np

D_MODEL = 1024
BATCH = 1
SEQ = 512
DEPTH = 1
DEC_BATCH = 1
DEC_SEQ = 2048
PAST_LEN = 128

HEAD_DIM = 64
N_HEADS = 8
N_KV_HEADS = 2
ATTN_W = N_HEADS * HEAD_DIM
KV_W = N_KV_HEADS * HEAD_DIM
CONV_W = D_MODEL - ATTN_W
CONV_GROUPS = 8
CONV_K = 31
WINDOW = 128
BLOCK = 128
D_FF = 2816
FFN_CONV_K = 3
IN_W = ATTN_W + 2 * KV_W + 2 * CONV_W
NEG_INF = -1e30

kernel_name = "hymba_swa_conformer_convffn_encoder"

def _rms(x, g, eps=1e-6):
    xf = x.astype(jnp.float32)
    y = xf * lax.rsqrt(jnp.mean(xf * xf, axis=-1, keepdims=True) + eps)
    return (y * g.astype(jnp.float32)).astype(x.dtype)

def _layernorm(x, g, b, eps=1e-5):
    xf = x.astype(jnp.float32)
    mu = jnp.mean(xf, axis=-1, keepdims=True)
    var = jnp.mean(jnp.square(xf - mu), axis=-1, keepdims=True)
    y = (xf - mu) * lax.rsqrt(var + eps)
    return (y * g.astype(jnp.float32) + b.astype(jnp.float32)).astype(x.dtype)

def _dwconv(x, w, b):
    K, C = w.shape
    y = lax.conv_general_dilated(
        x, w[:, None, :].astype(x.dtype), window_strides=(1,),
        padding=[(K // 2, K // 2)], dimension_numbers=("NWC", "WIO", "NWC"),
        feature_group_count=C)
    return y + b.astype(x.dtype)

def _alibi_slopes(n):
    return jnp.asarray(np.array([2.0 ** (-8.0 * (h + 1) / n) for h in range(n)], dtype=np.float32))

def _window_attention(q, k, v, sink):
    B, T, H, hd = q.shape
    KVH = k.shape[2]
    G = H // KVH
    nb = T // BLOCK
    qb = q.reshape(B, nb, BLOCK, KVH, G, hd).astype(jnp.float32)

    def band(t):
        tb = t.reshape(B, nb, BLOCK, KVH, hd)
        tp = jnp.pad(tb, ((0, 0), (1, 1), (0, 0), (0, 0), (0, 0)))
        return jnp.concatenate([tp[:, :-2], tp[:, 1:-1], tp[:, 2:]], axis=2)

    kb = band(k).astype(jnp.float32)
    vb = band(v)
    s = jnp.einsum("bnqkgd,bnskd->bnkgqs", qb, kb) * (hd ** -0.5)

    blk = jnp.arange(nb)[:, None]
    qpos = blk * BLOCK + jnp.arange(BLOCK)[None, :]
    kpos = (blk - 1) * BLOCK + jnp.arange(3 * BLOCK)[None, :]
    dist = jnp.abs(qpos[:, :, None] - kpos[:, None, :])
    valid = (dist <= WINDOW) & (kpos[:, None, :] >= 0) & (kpos[:, None, :] < T)
    slopes = _alibi_slopes(H).reshape(KVH, G)
    bias = -slopes[None, :, :, None, None] * dist[:, None, None].astype(jnp.float32)
    s = jnp.where(valid[:, None, None], s + bias[None], NEG_INF)

    sink_col = jnp.broadcast_to(sink.astype(jnp.float32).reshape(1, 1, KVH, G, 1, 1), s.shape[:-1] + (1,))
    p = jax.nn.softmax(jnp.concatenate([s, sink_col], axis=-1), axis=-1)[..., :-1]
    o = jnp.einsum("bnkgqs,bnskd->bnqkgd", p.astype(v.dtype), vb)
    return o.reshape(B, T, H * hd)

def _layer(x, norm1_g, w_in, q_norm_g, k_norm_g, attn_sink, conv_dw_w, conv_dw_b,
           conv_ln_g, conv_ln_b, w_out, norm2_g, ffn_w_gate, ffn_w_up, ffn_dw_w,
           ffn_dw_b, ffn_w_down):
    B, T, _ = x.shape
    h = _rms(x, norm1_g)
    proj = h @ w_in
    q, k, v, c = jnp.split(proj, [ATTN_W, ATTN_W + KV_W, ATTN_W + 2 * KV_W], axis=-1)
    q = _rms(q.reshape(B, T, N_HEADS, HEAD_DIM), q_norm_g)
    k = _rms(k.reshape(B, T, N_KV_HEADS, HEAD_DIM), k_norm_g)
    v = v.reshape(B, T, N_KV_HEADS, HEAD_DIM)
    attn = _window_attention(q, k, v, attn_sink)
    a, gate = jnp.split(c, 2, axis=-1)
    u = a * jax.nn.sigmoid(gate)
    u = _dwconv(u, conv_dw_w, conv_dw_b)
    u = jax.nn.silu(_layernorm(u, conv_ln_g, conv_ln_b))
    x = x + jnp.concatenate([attn, u], axis=-1) @ w_out
    h2 = _rms(x, norm2_g)
    g = jax.nn.silu(_dwconv(h2 @ ffn_w_gate, ffn_dw_w, ffn_dw_b))
    x = x + (g * (h2 @ ffn_w_up)) @ ffn_w_down
    return x

def _trunk(x, norm1_g, w_in, q_norm_g, k_norm_g, attn_sink, conv_dw_w, conv_dw_b,
           conv_ln_g, conv_ln_b, w_out, norm2_g, ffn_w_gate, ffn_w_up, ffn_dw_w,
           ffn_dw_b, ffn_w_down):
    for l in range(DEPTH):
        x = _layer(x, norm1_g[l], w_in[l], q_norm_g[l], k_norm_g[l], attn_sink[l],
                   conv_dw_w[l], conv_dw_b[l], conv_ln_g[l], conv_ln_b[l], w_out[l],
                   norm2_g[l], ffn_w_gate[l], ffn_w_up[l], ffn_dw_w[l], ffn_dw_b[l],
                   ffn_w_down[l])
    return x

def setup_inputs(seed: int = 0) -> dict:
    key = jax.random.key(seed)
    ks = jax.random.split(key, 20)
    f32 = jnp.float32
    nrm = lambda k, shape, s: jax.random.normal(k, shape, dtype=f32) * s
    L = DEPTH
    return {
        "x_prompt": nrm(ks[0], (BATCH, SEQ, D_MODEL), 1.0),
        "x_sample": nrm(ks[1], (DEC_BATCH, DEC_SEQ, D_MODEL), 1.0),
        "norm1_g": 1.0 + nrm(ks[2], (L, D_MODEL), 0.02),
        "w_in": nrm(ks[3], (L, D_MODEL, IN_W), D_MODEL ** -0.5),
        "q_norm_g": 1.0 + nrm(ks[4], (L, HEAD_DIM), 0.02),
        "k_norm_g": 1.0 + nrm(ks[5], (L, HEAD_DIM), 0.02),
        "attn_sink": nrm(ks[6], (L, N_HEADS), 0.5),
        "conv_dw_w": nrm(ks[7], (L, CONV_K, CONV_W), CONV_K ** -0.5),
        "conv_dw_b": nrm(ks[8], (L, CONV_W), 0.02),
        "conv_ln_g": 1.0 + nrm(ks[9], (L, CONV_W), 0.02),
        "conv_ln_b": nrm(ks[10], (L, CONV_W), 0.02),
        "w_out": nrm(ks[11], (L, D_MODEL, D_MODEL), D_MODEL ** -0.5),
        "norm2_g": 1.0 + nrm(ks[12], (L, D_MODEL), 0.02),
        "ffn_w_gate": nrm(ks[13], (L, D_MODEL, D_FF), D_MODEL ** -0.5),
        "ffn_w_up": nrm(ks[14], (L, D_MODEL, D_FF), D_MODEL ** -0.5),
        "ffn_dw_w": nrm(ks[15], (L, FFN_CONV_K, D_FF), FFN_CONV_K ** -0.5),
        "ffn_dw_b": nrm(ks[16], (L, D_FF), 0.02),
        "ffn_w_down": nrm(ks[17], (L, D_FF, D_MODEL), D_FF ** -0.5),
    }

def reference(x_prompt, x_sample, norm1_g, w_in, q_norm_g, k_norm_g, attn_sink, conv_dw_w,
              conv_dw_b, conv_ln_g, conv_ln_b, w_out, norm2_g, ffn_w_gate, ffn_w_up,
              ffn_dw_w, ffn_dw_b, ffn_w_down):
    y_prompt = _trunk(x_prompt, norm1_g, w_in, q_norm_g, k_norm_g, attn_sink, conv_dw_w,
                      conv_dw_b, conv_ln_g, conv_ln_b, w_out, norm2_g, ffn_w_gate, ffn_w_up,
                      ffn_dw_w, ffn_dw_b, ffn_w_down)
    y_sample = _trunk(x_sample, norm1_g, w_in, q_norm_g, k_norm_g, attn_sink, conv_dw_w,
                      conv_dw_b, conv_ln_g, conv_ln_b, w_out, norm2_g, ffn_w_gate, ffn_w_up,
                      ffn_dw_w, ffn_dw_b, ffn_w_down)
    return (y_prompt, y_sample)


_drawn_inputs = setup_inputs


def setup_inputs(seed=0):
    import zlib

    import numpy as np

    out = dict(_drawn_inputs(seed))
    spreads = {}
    factors = {'norm1_g': 5.109,
     'q_norm_g': 8.0,
     'k_norm_g': 8.0,
     'attn_sink': 4.739,
     'conv_dw_b': 11.722,
     'conv_ln_g': 19.151,
     'conv_ln_b': 17.843,
     'norm2_g': 4.075,
     'ffn_dw_b': 5.963}
    for name, (base, spread) in spreads.items():
        noise = np.random.default_rng([zlib.crc32(name.encode()), seed]).standard_normal(out[name].shape)
        drawn = base * np.exp(spread * noise) if base else spread * noise
        out[name] = __import__('jax').numpy.asarray(drawn.astype(out[name].dtype))
    for name, factor in factors.items():
        out[name] = (out[name] * factor).astype(out[name].dtype)
    return out
```

```python
from contextlib import ExitStack

import numpy as np
import concourse.bass as bass
from concourse import mybir

F32 = mybir.dt.float32
F32R = mybir.dt.float32r
ALU = mybir.AluOpType
ACT = mybir.ActivationFunctionType

P = 128
D_MODEL = 1024
PROMPT, SAMPLE = 512, 2048
TOKENS = PROMPT + SAMPLE
HEADS, KV_HEADS, HEAD_DIM = 8, 2, 64
GROUP = HEADS // KV_HEADS
ATTN_W = HEADS * HEAD_DIM
KV_W = KV_HEADS * HEAD_DIM
CONV_W = D_MODEL - ATTN_W
TAPS = 31
HALO = TAPS // 2
WINDOW = 128
D_FF = 2816
FFN_TAPS = 3

KT = D_MODEL // P
CT = CONV_W // P
FT = D_FF // P
AT = ATTN_W // P

TA = 256
STEPS = TOKENS // TA
PROJ = 2 * CT + 2 + AT
F_V, F_K = 2 * CT, 2 * CT + 1
NORMED = 1 + AT
PROJ_BANKS = 4

TB = 512
CHUNKS = TOKENS // TB
BLOCKS = TB // P
UNITS = BLOCKS * KV_HEADS
BAND = 3 * P

CONV_LAG = 3
PAIRS = CHUNKS * CT // 2
PAIR_OPS = 2 * TAPS
PROMPT_U = PROMPT + 2 * HALO
U_COLS = PROMPT_U + SAMPLE + 2 * HALO

TC = 428
WINDOWS = 6
OUT_COLS = TC * WINDOWS
PAD_COLS = OUT_COLS + 2
PAD_SPANS = ((0, 1), (1 + PROMPT, 1), (2 + TOKENS, PAD_COLS - TOKENS - 2))
ZERO_STORES = 4 + 2 * len(PAD_SPANS)
TH = TC + 2
W_PIECE = 8
DOWN_PIECES = -(-FT // W_PIECE)
TILES_F = 2 * FT
TILES_D = KT * DOWN_PIECES
TILES_W = TILES_F + TILES_D
RING = 4

NEG = -1e30

PARAM_SPLIT = [("g1", KT), ("g2", KT), ("conv_w", CT * TAPS), ("conv_b", CT), ("ln_g", CT), ("ln_b", CT),
               ("ffn_w", FT * FFN_TAPS), ("ffn_b", FT), ("q_g", 1), ("k_g", 1), ("sink", HEADS)]
PARAM_AT = {}
PARAM_COLS = 0
for _name, _n in PARAM_SPLIT:
    PARAM_AT[_name] = PARAM_COLS
    PARAM_COLS += _n


def padded(c):
    return 1 + TB * c + (1 if TB * c >= PROMPT else 0)


def u_window(c):
    return 0 if c == 0 else PROMPT_U + TB * (c - 1)


def u_column(t):
    return HALO + TA * t if TA * t < PROMPT else PROMPT_U + HALO + TA * t - PROMPT


def unit_last_op(unit):
    return PAIR_OPS * (unit // 2) + PAIR_OPS - 2 + unit % 2


def encoder_layer(nc, x, w_in, w_out, w_ffn, w_down, params, consts, y):
    with ExitStack() as ctx:
        def dram(name, shape):
            return nc.dram_tensor(name, shape, F32, kind="Internal").ap()

        q_d = dram("q_scratch", (AT, P, TOKENS))
        k_d = dram("k_scratch", (P, TOKENS))
        v_d = dram("v_scratch", (TOKENS // P, P, KV_W))
        u_d = dram("u_scratch", (CT, P, U_COLS))
        c_d = dram("conv_scratch", (CT, P, TOKENS))
        x2_d = dram("x2_scratch", (KT, P, PAD_COLS))
        h2_d = dram("h2_scratch", (KT, P, PAD_COLS))

        def sb(stack, name, shape, dt=F32):
            return stack.enter_context(nc.sbuf_tensor(name, shape, dt))

        def sem(name):
            return ctx.enter_context(nc.semaphore(name))

        bank = [ctx.enter_context(nc.psum_tensor(f"bank{i}", [P, 512], F32)) for i in range(8)]

        par = sb(ctx, "par", [P, PARAM_COLS])
        ones = sb(ctx, "ones", [P, P])
        halves = sb(ctx, "halves", [P, P])
        ident = sb(ctx, "ident", [P, P])
        eps = sb(ctx, "eps", [P, 2])
        qg = sb(ctx, "qg", [P, 1])
        zeros = sb(ctx, "zeros", [P, max(CT * HALO, KT * PAD_SPANS[-1][1])])

        def col(name, i=0):
            return par[:, PARAM_AT[name] + i:PARAM_AT[name] + i + 1]

        ffn_w_ap = par[:, PARAM_AT["ffn_w"]:PARAM_AT["ffn_w"] + FT * FFN_TAPS]

        ab = ctx.enter_context(ExitStack())
        conv_win = [sb(ab, f"conv_win{i}", [P, TB + 2 * HALO]) for i in range(4)]
        conv_acc = [sb(ab, f"conv_acc{i}", [P, TB]) for i in range(4)]

        a = ExitStack()
        win_hi = sb(a, "win_hi", [P, PROJ, KT, P], F32R)
        win_lo = sb(a, "win_lo", [P, PROJ, KT, P], F32R)
        h_hi = [sb(a, "h_hi0", [P, KT, TA], F32R)]
        h_lo = [sb(a, "h_lo0", [P, KT, TA], F32R)]
        with ExitStack() as start:
            w_raw = [sb(start, f"w_raw{i}", [P, KT * P])[:] for i in range(4)]
        h_hi.append(sb(a, "h_hi1", [P, KT, TA], F32R))
        h_lo.append(sb(a, "h_lo1", [P, KT, TA], F32R))
        xs = [sb(a, f"xs{i}", [P, KT, TA]) for i in range(2)]
        hb = sb(a, "hb", [P, KT, TA])
        n_rms = sb(a, "n_rms", [P, TA])
        n_inv = sb(a, "n_inv", [P, TA])
        sig = [sb(a, f"sig{i}", [P, TA]) for i in range(2)]
        ub = [sb(a, f"ub{i}", [P, TA]) for i in range(2)]
        vb = sb(a, "vb", [P, TA])
        q_raw = [sb(a, f"q_raw{i}", [P, TA]) for i in range(2)]
        q_sq = [sb(a, f"q_sq{i}", [P, TA]) for i in range(2)]
        q_rms = [sb(a, f"q_rms{i}", [P, TA]) for i in range(2)]
        q_inv = [sb(a, f"q_inv{i}", [P, TA]) for i in range(2)]
        q_nrm = [sb(a, f"q_nrm{i}", [P, TA]) for i in range(2)]
        a.close()

        b = ExitStack()
        wo_hi = sb(b, "wo_hi", [P, KT, KT, P], F32R)
        wo_lo = sb(b, "wo_lo", [P, KT, KT, P], F32R)
        qw = sb(b, "qw", [P, AT, TB])
        kw = sb(b, "kw", [P, TB + 2 * P])
        vw = sb(b, "vw", [P, BLOCKS + 2, KV_W])
        cc = sb(b, "cc", [P, CT, TB])
        xb = sb(b, "xb", [P, KT, TB])
        cat_hi = sb(b, "cat_hi", [P, KT, TB], F32R)
        cat_lo = sb(b, "cat_lo", [P, KT, TB], F32R)
        bias = sb(b, "bias", [P, HEADS, BAND])
        S = [sb(b, f"S{i}", [P, GROUP, BAND]) for i in range(2)]
        PT = [sb(b, f"PT{i}", [P, 3, TB]) for i in range(2)]
        sq = [sb(b, f"sq{i}", [P, TB]) for i in range(2)]
        h2b = [sb(b, f"h2b{i}", [P, TB]) for i in range(2)]
        st_a = sb(b, "st_a", [P, TB])
        st_b = sb(b, "st_b", [P, TB])
        n2_rms = sb(b, "n2_rms", [P, TB])
        n2_inv = sb(b, "n2_inv", [P, TB])
        mx = [sb(b, f"mx{i}", [P, GROUP]) for i in range(2)]
        m4 = [sb(b, f"m4{i}", [P, GROUP]) for i in range(2)]
        nm4 = [sb(b, f"nm4{i}", [P, GROUP]) for i in range(2)]
        es4 = [sb(b, f"es4{i}", [P, GROUP]) for i in range(2)]
        rs4 = [sb(b, f"rs4{i}", [P, GROUP]) for i in range(2)]
        ee4 = [sb(b, f"ee4{i}", [P, GROUP]) for i in range(2)]
        dn4 = [sb(b, f"dn4{i}", [P, GROUP]) for i in range(2)]
        ri4 = [sb(b, f"ri4{i}", [P, GROUP]) for i in range(2)]
        wo_raw = [t[:].rearrange("p h s -> p (h s)")[:, 0:KT * P] for t in S]
        b.close()
        ab.close()

        c_ = ctx.enter_context(ExitStack())
        mid_hi = sb(c_, "mid_hi", [P, FT * TC], F32R)
        mid_lo = sb(c_, "mid_lo", [P, FT * TC], F32R)
        hw_hi = sb(c_, "hw_hi", [P, KT, TH], F32R)
        hw_lo = sb(c_, "hw_lo", [P, KT, TH], F32R)
        hw_raw = sb(c_, "hw_raw", [P, KT, TH])
        wraw = [sb(c_, f"wraw{i}", [P, W_PIECE, P]) for i in range(RING)]
        whi = [sb(c_, f"whi{i}", [P, W_PIECE, P], F32R) for i in range(RING)]
        wlo = [sb(c_, f"wlo{i}", [P, W_PIECE, P], F32R) for i in range(RING)]
        gb = [sb(c_, f"gb{i}", [P, TH]) for i in range(2)]
        cv = [sb(c_, f"cv{i}", [P, TC]) for i in range(2)]
        mb = [sb(c_, f"mb{i}", [P, TC]) for i in range(2)]
        x2w = [sb(c_, f"x2w{i}", [P, TC]) for i in range(2)]
        yb = [sb(c_, f"yb{i}", [P, TC]) for i in range(2)]

        s_par = sem("params_loaded")
        s_set = sem("constants_set")
        s_zst = sem("pads_stored")
        s_x = [sem(f"x_loaded{i}") for i in range(2)]
        s_wr = [sem(f"w_in_loaded{i}") for i in range(4)]
        s_whi = sem("w_in_hi_ready")
        s_wlo = sem("w_in_lo_ready")
        s_xsq = sem("x_squared")
        s_nst = sem("norm1_sum_ready")
        s_nrt = sem("norm1_root_ready")
        s_nin = sem("norm1_inverse_ready")
        s_hf = sem("h_ready")
        s_hhi = sem("h_hi_ready")
        s_hlo = sem("h_lo_ready")
        s_pj = sem("projection_ready")
        s_sig = sem("glu_sigmoid_ready")
        s_u = sem("glu_ready")
        s_ust = [sem(f"glu_stored{i}") for i in range(2)]
        s_v = sem("v_ready")
        s_vst = sem("v_stored")
        s_qs = sem("qk_squared")
        s_qr = sem("qk_copied")
        s_qss = sem("qk_sum_ready")
        s_qrt = sem("qk_root_ready")
        s_qin = sem("qk_inverse_ready")
        s_qn = sem("qk_normed")
        s_qst = [sem(f"qk_stored{i}") for i in range(2)]
        s_win = [sem(f"conv_window_loaded{i}") for i in range(4)]
        s_cv = sem("conv_step_done")
        s_cst = [sem(f"conv_stored{i}") for i in range(4)]

        s_bias = sem("bias_loaded")
        s_wor = [sem(f"w_out_loaded{i}") for i in range(2)]
        s_wohi = sem("w_out_hi_ready")
        s_wolo = sem("w_out_lo_ready")
        s_qkv = sem("qkv_loaded")
        s_cc = sem("conv_loaded")
        s_xb = sem("residual_loaded")
        s_l = {k: sem(f"ln_{k}") for k in ("sum", "mean", "centred", "var", "root", "inverse", "scaled",
                                           "swish", "hi", "lo")}
        s_lsq = sem("ln_squared")
        s_qk = sem("scores_ready")
        s_sb = sem("scores_biased")
        s_m4 = sem("max_ready")
        s_nm = sem("negmax_ready")
        s_es = sem("sink_shifted")
        s_ex = sem("exp_ready")
        s_ee = sem("sink_exp_ready")
        s_dn = sem("denominator_ready")
        s_ri = sem("inverse_denominator_ready")
        s_p = sem("probs_ready")
        s_t = sem("probs_transposed")
        s_ta = sem("probsT_copied_by_act")
        s_tv = sem("probsT_copied_by_dve")
        s_pv = sem("attention_ready")
        s_ahi = sem("attention_hi_ready")
        s_alo = sem("attention_lo_ready")
        s_wo = sem("out_projection_ready")
        s_x2 = sem("x2_ready")
        s_x2q = sem("x2_squared")
        s_n2m = sem("norm2_term_added")
        s_n2r = sem("norm2_root_ready")
        s_n2i = sem("norm2_inverse_ready")
        s_h2 = sem("h2_ready")
        s_x2st = sem("x2_stored")
        s_h2st = [sem(f"h2_stored{i}") for i in range(2)]

        s_hw = sem("window_loaded")
        s_hwhi = sem("window_hi_ready")
        s_hwlo = sem("window_lo_ready")
        s_rw = [sem(f"ffn_weight_loaded{i}") for i in range(RING)]
        s_fhi = sem("ffn_weight_hi_ready")
        s_flo = sem("ffn_weight_lo_ready")
        s_used = sem("ffn_products_done")
        s_gb = sem("gate_copied")
        s_c1 = sem("ffn_tap1_done")
        s_c2 = sem("ffn_tap2_done")
        s_c3 = sem("ffn_conv_ready")
        s_sl = sem("ffn_swish_ready")
        s_m = sem("mid_ready")
        s_mhi = sem("mid_hi_ready")
        s_mlo = sem("mid_lo_ready")
        s_x2w = [sem(f"residual_window_loaded{i}") for i in range(2)]
        s_y = sem("y_ready")
        s_yst = [sem(f"y_stored{i}") for i in range(2)]

        block = ctx.enter_context(nc.Block())

        def kts(c, n):
            first = n == 0 and c in (0, 1)
            last = n == BLOCKS - 1 and c in (0, CHUNKS - 1)
            return [k for k in range(3) if not (k == 0 and first) and not (k == 2 and last)]

        t_seq, acts, dves = {}, {}, {}
        n_act = n_dve = 0
        for c in range(CHUNKS):
            for u in range(UNITS):
                ks = kts(c, u // KV_HEADS)
                for kt in ks:
                    t_seq[UNITS * c + u, kt] = len(t_seq)
                    by_dve = kt == ks[-1]
                    n_dve += by_dve
                    n_act += not by_dve
                    acts[UNITS * c + u, kt] = (by_dve, n_dve if by_dve else n_act)
        t_list = list(t_seq)

        def wait_copied(eng, U, kt):
            by_dve, count = acts[U, kt]
            eng.wait_ge(s_tv if by_dve else s_ta, count)

        @block.sync
        def _(sp):
            def load_x(t):
                if t >= 2:
                    sp.wait_ge(s_hf, KT * (t - 1))
                sp.dma_start(xs[t % 2][:], x[:, :, TA * t:TA * (t + 1)]).then_inc(s_x[t % 2], 16)

            def load_window(unit):
                c, j = divmod(unit, CT)
                if unit >= 4:
                    sp.wait_ge(s_cv, unit_last_op(unit - 4) + 1)
                sp.dma_start(conv_win[unit % 4][:], u_d[j, :, u_window(c):u_window(c) + TB + 2 * HALO]) \
                  .then_inc(s_win[unit % 4], 16)

            def store_conv(unit):
                c, j = divmod(unit, CT)
                sp.wait_ge(s_cv, unit_last_op(unit) + 1)
                sp.dma_start(c_d[j, :, TB * c:TB * (c + 1)], conv_acc[unit % 4][:]).then_inc(s_cst[unit % 4], 16)

            def store_qk(t, m):
                M = NORMED * t + m
                sp.wait_ge(s_qn, M + 1)
                dst = k_d if m == 0 else q_d[m - 1]
                sp.dma_start(dst[:, TA * t:TA * (t + 1)], q_nrm[M % 2][:]).then_inc(s_qst[M % 2], 16)

            load_x(0)
            sp.dma_start(par[:], params).then_inc(s_par, 16)
            sp.dma_start(ones[:], consts[:, 0:P]).then_inc(s_par, 16)
            sp.dma_start(halves[:], consts[:, P:2 * P]).then_inc(s_par, 16)
            sp.dma_start(ident[:], consts[:, 2 * P:3 * P]).then_inc(s_par, 16)
            for f in range(PROJ):
                if f >= 4:
                    sp.wait_ge(s_wlo, f - 3)
                sp.dma_start(w_raw[f % 4], w_in[f].rearrange("p k n -> p (k n)")).then_inc(s_wr[f % 4], 16)
            load_x(1)
            sp.wait_ge(s_set, 1)
            z = zeros[:, 0:CT * HALO].rearrange("p (j n) -> p j n", j=CT)
            u_v = u_d.rearrange("j p n -> p j n")
            for at in (0, PROMPT_U - HALO, PROMPT_U, U_COLS - HALO):
                sp.dma_start(u_v[:, :, at:at + HALO], z).then_inc(s_zst, 16)
            for d in (x2_d, h2_d):
                dv = d.rearrange("k p n -> p k n")
                for at, n in PAD_SPANS:
                    sp.dma_start(dv[:, :, at:at + n], zeros[:, 0:KT * n].rearrange("p (k n) -> p k n", k=KT),
                                 allow_slow_non_contiguous=True).then_inc(s_zst, 16)

            for t in range(STEPS):
                if t > 0:
                    store_qk(t - 1, NORMED - 1)
                if 1 <= t and t + 1 < STEPS:
                    load_x(t + 1)
                for j in range(CT):
                    sp.wait_ge(s_u, CT * t + j + 1)
                    sp.dma_start(u_d[j, :, u_column(t):u_column(t) + TA], ub[j % 2][:]).then_inc(s_ust[j % 2], 16)
                sp.wait_ge(s_v, t + 1)
                sp.dma_start(v_d[2 * t:2 * t + 2].rearrange("n p d -> p n d"),
                             vb[:].rearrange("p (n d) -> p n d", n=2)).then_inc(s_vst, 16)
                store_qk(t, 0)
                store_qk(t, 1)
                pair = t - CONV_LAG + 1
                if 0 <= pair < PAIRS:
                    sp.wait_ge(s_ust[0], 16 * (CT // 2) * (t + 1))
                    sp.wait_ge(s_ust[1], 16 * (CT // 2) * (t + 1))
                    if pair == 0:
                        sp.wait_ge(s_zst, 16 * ZERO_STORES)
                    load_window(2 * pair)
                    load_window(2 * pair + 1)
                store_qk(t, 2)
                store_qk(t, 3)
                if t >= CONV_LAG:
                    store_conv(2 * (t - CONV_LAG))
                    store_conv(2 * (t - CONV_LAG) + 1)
            store_qk(STEPS - 1, NORMED - 1)

            done_pairs = STEPS - CONV_LAG

            sp.wait_ge(s_pj, PROJ * STEPS)
            sp.wait_ge(s_vst, 16 * STEPS)
            for i in range(2):
                sp.wait_ge(s_qst[i], 16 * NORMED * STEPS // 2)
            sp.dma_start(bias[:], consts[:, 3 * P:].rearrange("p (h s) -> p h s", h=HEADS)).then_inc(s_bias, 16)

            def load_qkv(c):
                if c > 0:
                    sp.wait_ge(s_qk, GROUP * UNITS * c)
                    sp.wait_ge(s_pv, UNITS * c)
                sp.dma_start(qw[:], q_d.rearrange("t p n -> p t n")[:, :, TB * c:TB * (c + 1)]).then_inc(s_qkv, 16)
                first, last = c in (0, 1), c in (0, CHUNKS - 1)
                n0, n1 = (0 if not first else 1), BLOCKS + 2 - (1 if last else 0)
                t0 = BLOCKS * c - 1
                sp.dma_start(kw[:, P * n0:P * n1], k_d[:, P * (t0 + n0):P * (t0 + n1)]).then_inc(s_qkv, 16)
                sp.dma_start(vw[:, n0:n1, :], v_d[t0 + n0:t0 + n1].rearrange("n p d -> p n d")).then_inc(s_qkv, 16)

            def load_cc(c):
                for j in range(CT):
                    sp.wait_ge(s_cst[j], 16 * (c + 1))
                if c > 0:
                    sp.wait_ge(s_l["lo"], c)
                sp.dma_start(cc[:], c_d.rearrange("j p n -> p j n")[:, :, TB * c:TB * (c + 1)]).then_inc(s_cc, 16)

            load_cc(0)
            load_qkv(0)
            for o in range(KT):
                if o >= 2:
                    sp.wait_ge(s_wolo, o - 1)
                sp.dma_start(wo_raw[o % 2], w_out[o].rearrange("p k n -> p (k n)")).then_inc(s_wor[o % 2], 16)
            sp.dma_start(xb[:], x[:, :, 0:TB]).then_inc(s_xb, 16)
            for c in range(CHUNKS):
                pair = done_pairs + c
                if pair < PAIRS:
                    if c > 0:
                        load_window(2 * pair)
                        load_window(2 * pair + 1)
                if c + 1 < CHUNKS:
                    load_cc(c + 1)
                    load_qkv(c + 1)
                sp.wait_ge(s_x2, KT * (c + 1))
                sp.dma_start(x2_d.rearrange("k p n -> p k n")[:, :, padded(c):padded(c) + TB], xb[:]) \
                  .then_inc(s_x2st, 16)
                if pair < PAIRS:
                    store_conv(2 * pair)
                    store_conv(2 * pair + 1)
                for k in range(KT):
                    sp.wait_ge(s_h2, KT * c + k + 1)
                    sp.dma_start(h2_d[k, :, padded(c):padded(c) + TB], h2b[k % 2][:]).then_inc(s_h2st[k % 2], 16)
                if c + 1 < CHUNKS:
                    sp.wait_ge(s_x2st, 16 * (c + 1))
                    sp.dma_start(xb[:], x[:, :, TB * (c + 1):TB * (c + 2)]).then_inc(s_xb, 16)

            sp.wait_ge(s_x2st, 16 * CHUNKS)
            for i in range(2):
                sp.wait_ge(s_h2st[i], 16 * KT // 2 * CHUNKS)
            sp.wait_ge(s_wo, KT * CHUNKS)

            def load_h(w):
                sp.dma_start(hw_raw[:], h2_d.rearrange("k p n -> p k n")[:, :, TC * w:TC * w + TH]).then_inc(s_hw, 16)

            def load_weight(n, slot, src):
                sp.wait_ge(s_flo, n + 1)
                sp.dma_start(wraw[slot][:], src).then_inc(s_rw[slot], 16)

            load_h(0)
            for w in range(WINDOWS):
                base = TILES_W * w
                with sp.Fori(0, FT // 2) as i:
                    for s in range(4):
                        load_weight(base + 4 * i + s, s, w_ffn[bass.ds(4 * i + s, 1)].rearrange("o p k n -> (o p) k n"))
                for o in range(KT):
                    for s in range(DOWN_PIECES):
                        n = DOWN_PIECES * o + s
                        load_weight(base + TILES_F + n, n % RING, w_down[o, s])
                    if KT * w + o >= 2:
                        sp.wait_ge(s_y, KT * w + o - 1)
                    sp.dma_start(x2w[o % 2][:], x2_d[o, :, 1 + TC * w:1 + TC * (w + 1)]).then_inc(s_x2w[o % 2], 16)
                    if o == 1 and w + 1 < WINDOWS:
                        sp.wait_ge(s_hwlo, w + 1)
                        load_h(w + 1)
            for i in range(2):
                sp.wait_ge(s_yst[i], 16 * WINDOWS * KT // 2)

        @block.scalar
        def _(act):
            def square_x(t):
                act.wait_ge(s_x[t % 2], 16 * (t // 2 + 1))
                if t > 0:
                    act.wait_ge(s_hlo, t)
                nc.scalar.activation(hb[:], xs[t % 2][:], ACT.Square).then_inc(s_xsq, 1)

            def norm_root(t):
                act.wait_ge(s_nst, t + 1)
                nc.scalar.activation(n_rms[:], bank[7][:, 0:TA], ACT.Sqrt, bias=eps[:, 0:1],
                                     scale=1.0 / D_MODEL).then_inc(s_nrt, 1)

            def h_high(t):
                act.wait_ge(s_hf, KT * (t + 1))
                if t >= 2:
                    act.wait_ge(s_pj, PROJ * (t - 1))
                if t == 1:
                    act.wait_ge(s_wlo, PROJ)
                nc.scalar.activation(h_hi[t % 2][:], hb[:], ACT.Copy).then_inc(s_hhi, 1)

            def qk_square(t, m):
                M = NORMED * t + m
                act.wait_ge(s_pj, PROJ * t + F_K + m + 1)
                if M >= 2:
                    act.wait_ge(s_qss, M - 1)
                nc.scalar.activation(q_sq[M % 2][:], bank[(PROJ * t + F_K + m) % PROJ_BANKS][:, 0:TA],
                                     ACT.Square).then_inc(s_qs, 1)

            def qk_root(t, m):
                M = NORMED * t + m
                act.wait_ge(s_qss, M + 1)
                if M >= 2:
                    act.wait_ge(s_qin, M - 1)
                nc.scalar.activation(q_rms[M % 2][:], bank[4 + M % 2][:, 0:TA], ACT.Sqrt, bias=eps[:, 0:1],
                                     scale=1.0 / HEAD_DIM).then_inc(s_qrt, 1)

            act.wait_ge(s_set, 4)
            square_x(0)
            act.wait_ge(s_wr[0], 16)
            nc.scalar.activation(win_hi[:, 0].rearrange("p k n -> p (k n)"), w_raw[0], ACT.Copy).then_inc(s_whi, 1)
            norm_root(0)
            h_high(0)
            for f in range(1, PROJ):
                act.wait_ge(s_wr[f % 4], 16 * (f // 4 + 1))
                nc.scalar.activation(win_hi[:, f].rearrange("p k n -> p (k n)"), w_raw[f % 4], ACT.Copy) \
                  .then_inc(s_whi, 1)
            for t in range(STEPS):
                if t > 0:
                    qk_root(t - 1, NORMED - 1)
                if t + 1 < STEPS:
                    square_x(t + 1)
                for j in range(CT):
                    n = PROJ * t + 2 * j + 1
                    act.wait_ge(s_pj, n + 1)
                    if CT * t + j >= 2:
                        act.wait_ge(s_u, CT * t + j - 1)
                    nc.scalar.activation(sig[j % 2][:], bank[n % PROJ_BANKS][:, 0:TA], ACT.Sigmoid).then_inc(s_sig, 1)
                if t + 1 < STEPS:
                    norm_root(t + 1)
                n = PROJ * t + F_V
                act.wait_ge(s_pj, n + 1)
                if t > 0:
                    act.wait_ge(s_vst, 16 * t)
                nc.scalar.activation(vb[:], bank[n % PROJ_BANKS][:, 0:TA], ACT.Copy).then_inc(s_v, 1)
                if t + 1 < STEPS:
                    h_high(t + 1)
                qk_square(t, 0)
                for m in range(1, NORMED):
                    qk_square(t, m)
                    qk_root(t, m - 1)
            qk_root(STEPS - 1, NORMED - 1)

            def ln_mean(c):
                act.wait_ge(s_l["sum"], c + 1)
                if c > 0:
                    act.wait_ge(s_l["inverse"], c)
                nc.scalar.activation(st_a[:], bank[6][:], ACT.Copy, scale=1.0 / CONV_W).then_inc(s_l["mean"], 1)

            def ln_square(c, j):
                n = CT * c + j
                act.wait_ge(s_l["centred"], c + 1)
                if j < 2:
                    if c > 1:
                        act.wait_ge(s_n2m, KT * (c - 1))
                else:
                    act.wait_ge(s_l["var"], n - 1)
                nc.scalar.activation(sq[j % 2][:], cc[:, j, :], ACT.Square).then_inc(s_lsq, 1)

            def ln_root(c):
                act.wait_ge(s_l["var"], CT * (c + 1))
                nc.scalar.activation(st_a[:], bank[6][:], ACT.Sqrt, bias=eps[:, 1:2],
                                     scale=1.0 / CONV_W).then_inc(s_l["root"], 1)

            def ln_swish(c):
                act.wait_ge(s_l["scaled"], c + 1)
                for j in range(CT):
                    nc.scalar.activation(cc[:, j, :], cc[:, j, :], ACT.Silu, bias=col("ln_b", j),
                                         scale=col("ln_g", j)).then_inc(s_l["swish"], 1)

            def ln_high(c):
                act.wait_ge(s_l["swish"], CT * (c + 1))
                if c > 0:
                    act.wait_ge(s_wo, KT * c)
                nc.scalar.activation(cat_hi[:, AT:KT, :], cc[:], ACT.Copy).then_inc(s_l["hi"], 1)

            def exps(U):
                act.wait_ge(s_nm, U + 1)
                if U >= 2:
                    act.wait_ge(s_dn, U - 1)
                c, u = divmod(U, UNITS)
                ks = kts(c, u // KV_HEADS)
                for t in range(GROUP):
                    s_ = S[U % 2][:, t, P * ks[0]:P * (ks[-1] + 1)]
                    nc.scalar.activation(s_, s_, ACT.Exp, bias=nm4[U % 2][:, t:t + 1],
                                         accum_out=rs4[U % 2][:, t:t + 1]).then_inc(s_ex, 1)
                act.wait_ge(s_es, U + 1)
                nc.scalar.activation(ee4[U % 2][:], es4[U % 2][:], ACT.Exp).then_inc(s_ee, 1)

            def copy_t(U):
                c, u = divmod(U, UNITS)
                for kt in kts(c, u // KV_HEADS):
                    if acts[U, kt][0]:
                        continue
                    act.wait_ge(s_t, t_seq[U, kt] + 1)
                    if U >= 2:
                        act.wait_ge(s_pv, U - 1)
                    nc.scalar.activation(PT[U % 2][:, kt, :], bank[4 + t_seq[U, kt] % 2][:], ACT.Copy) \
                      .then_inc(s_ta, 1)

            def attn_high(U):
                c, u = divmod(U, UNITS)
                n, g = divmod(u, KV_HEADS)
                act.wait_ge(s_pv, U + 1)
                if u < 2 and c > 0:
                    act.wait_ge(s_wo, KT * c)
                rows = slice(HEAD_DIM * g, HEAD_DIM * (g + 1))
                nc.scalar.activation(cat_hi[rows, 0:AT, P * n:P * (n + 1)],
                                     bank[7][rows, :].rearrange("p (t q) -> p t q", t=AT), ACT.Copy) \
                  .then_inc(s_ahi, 1)

            act.wait_ge(s_cc, 16)
            ln_mean(0)
            for j in range(CT):
                ln_square(0, j)
            ln_root(0)
            for o in range(KT):
                act.wait_ge(s_wor[o % 2], 16 * (o // 2 + 1))
                nc.scalar.activation(wo_hi[:, o].rearrange("p k n -> p (k n)"), wo_raw[o % 2], ACT.Copy) \
                  .then_inc(s_wohi, 1)
            ln_swish(0)
            for c in range(CHUNKS):
                ln_high(c)
                if c == 0:
                    exps(0)
                for u in range(UNITS):
                    U = UNITS * c + u
                    if u > 0:
                        attn_high(U - 1)
                    copy_t(U)
                    if u + 1 < UNITS:
                        exps(U + 1)
                    if c + 1 < CHUNKS:
                        if u == 1:
                            ln_mean(c + 1)
                        if u == 3:
                            for j in range(CT):
                                ln_square(c + 1, j)
                        if u == 4:
                            ln_root(c + 1)
                        if u == 6:
                            ln_swish(c + 1)
                attn_high(UNITS * c + UNITS - 1)
                for o in range(KT):
                    n = KT * c + o
                    act.wait_ge(s_x2, n + 1)
                    if o >= 2:
                        act.wait_ge(s_n2m, n - 1)
                    elif c + 1 < CHUNKS:
                        act.wait_ge(s_l["var"], CT * (c + 2))
                    nc.scalar.activation(sq[o % 2][:], xb[:, o, :], ACT.Square).then_inc(s_x2q, 1)
                act.wait_ge(s_n2m, KT * (c + 1))
                nc.scalar.activation(n2_rms[:], bank[6][:], ACT.Sqrt, bias=eps[:, 0:1],
                                     scale=1.0 / D_MODEL).then_inc(s_n2r, 1)
                if c + 1 < CHUNKS:
                    exps(UNITS * (c + 1))

            def weight_high(n, slot, turn):
                act.wait_ge(s_rw[slot], 16 * (turn + 1))
                act.wait_ge(s_used, n + 1)
                nc.scalar.activation(whi[slot][:], wraw[slot][:], ACT.Copy).then_inc(s_fhi, 1)

            def window_high(w):
                act.wait_ge(s_hw, 16 * (w + 1))
                if w > 0:
                    act.wait_ge(s_used, RING + TILES_W * (w - 1) + TILES_F)
                nc.scalar.activation(hw_hi[:], hw_raw[:], ACT.Copy).then_inc(s_hwhi, 1)

            act.sem_inc(s_gb, 2)
            window_high(0)
            weight_high(0, 0, 0)
            weight_high(1, 1, 0)
            for w in range(WINDOWS):
                base = TILES_W * w
                turns = TILES_W // RING * w
                with act.Fori(0, FT // 2) as i:
                    for s in range(2):
                        J = FT * w + 2 * i + s
                        for r in range(2):
                            tile = 2 * s + 2 + r
                            weight_high(base + 4 * i + tile, tile % RING, turns + i + tile // RING)
                        act.wait_ge(s_used, RING + base + 4 * i + 2 * s + 1)
                        act.wait_ge(s_c3, J + 1)
                        nc.scalar.activation(gb[s][:], bank[s][:, 0:TH], ACT.Copy).then_inc(s_gb, 1)
                        act.wait_ge(s_c3, J + 3)
                        nc.scalar.activation(cv[s][:], cv[s][:], ACT.Silu).then_inc(s_sl, 1)
                        act.wait_ge(s_m, J + 3)
                        nc.scalar.activation(mid_hi[:, bass.ds((2 * i + s) * TC, TC)], mb[s][:], ACT.Copy) \
                          .then_inc(s_mhi, 1)
                for o in range(KT):
                    for s in range(DOWN_PIECES):
                        n = TILES_F + DOWN_PIECES * o + s + 2
                        if base + n < TILES_W * WINDOWS:
                            weight_high(base + n, n % RING, turns + n // RING)
                    if o > 0:
                        n = KT * w + o - 1
                        act.wait_ge(s_y, n + 1)
                        act.dma_start(y[o - 1, :, TC * w:TC * (w + 1)], yb[(o - 1) % 2][:]) \
                           .then_inc(s_yst[(o - 1) % 2], 16)
                    if o == 2 and w + 1 < WINDOWS:
                        window_high(w + 1)
                act.wait_ge(s_y, KT * (w + 1))
                act.dma_start(y[KT - 1, :, TC * w:TC * (w + 1)], yb[(KT - 1) % 2][:]).then_inc(s_yst[(KT - 1) % 2], 16)

        @block.gpsimd
        def _(pool):
            for t in range(STEPS):
                pool.wait_ge(s_hhi, t + 1)
                nc.gpsimd.tensor_tensor(h_lo[t % 2][:], hb[:], h_hi[t % 2][:].bitcast(F32), ALU.subtract) \
                  .then_inc(s_hlo, 1)
            for c in range(CHUNKS):
                pool.wait_ge(s_l["hi"], c + 1)
                nc.gpsimd.tensor_tensor(cat_lo[:, AT:KT, :], cc[:], cat_hi[:, AT:KT, :].bitcast(F32), ALU.subtract) \
                  .then_inc(s_l["lo"], 1)
            pool.sem_inc(s_flo, RING)

            def weight_low(n, slot):
                pool.wait_ge(s_fhi, n + 1)
                nc.gpsimd.tensor_tensor(wlo[slot][:], wraw[slot][:], whi[slot][:].bitcast(F32), ALU.subtract) \
                  .then_inc(s_flo, 1)

            def window_low(w):
                pool.wait_ge(s_hwhi, w + 1)
                nc.gpsimd.tensor_tensor(hw_lo[:], hw_raw[:], hw_hi[:].bitcast(F32), ALU.subtract).then_inc(s_hwlo, 1)

            window_low(0)
            for w in range(WINDOWS):
                base = TILES_W * w
                with pool.Fori(0, FT // 2) as i:
                    for s in range(RING):
                        weight_low(base + 4 * i + s, s)
                for n in range(TILES_D):
                    weight_low(base + TILES_F + n, n % RING)
                    if n == 3 * DOWN_PIECES + 1 and w + 1 < WINDOWS:
                        window_low(w + 1)

        @block.vector
        def _(dve):
            def conv_ops(first, count):
                for m in range(first, min(first + count, PAIRS * PAIR_OPS)):
                    pair, r = divmod(m, PAIR_OPS)
                    tap, unit = r // 2, 2 * pair + r % 2
                    j = unit % CT
                    win, acc = conv_win[unit % 4], conv_acc[unit % 4]
                    w_tap = par[:, PARAM_AT["conv_w"] + TAPS * j + tap:PARAM_AT["conv_w"] + TAPS * j + tap + 1]
                    if tap == 0:
                        dve.wait_ge(s_win[unit % 4], 16 * (unit // 4 + 1))
                        if unit >= 4:
                            dve.wait_ge(s_cst[unit % 4], 16 * (unit // 4))
                        nc.vector.tensor_scalar(acc[:], win[:, 0:TB], w_tap, col("conv_b", j), ALU.mult, ALU.add) \
                          .then_inc(s_cv, 1)
                    else:
                        dve.wait_ge(s_cv, m - 1)
                        nc.vector.scalar_tensor_tensor(acc[:], win[:, tap:tap + TB], w_tap, acc[:],
                                                       ALU.mult, ALU.add).then_inc(s_cv, 1)

            def conv_slot(t, i, slots):
                if t >= CONV_LAG:
                    lo, hi = PAIR_OPS * i // slots, PAIR_OPS * (i + 1) // slots
                    conv_ops(PAIR_OPS * (t - CONV_LAG) + lo, hi - lo)

            nc.vector.memset(zeros[:], 0.0).then_inc(s_set, 1)
            nc.vector.memset(eps[:, 0:1], 1e-6).then_inc(s_set, 1)
            nc.vector.memset(eps[:, 1:2], 1e-5).then_inc(s_set, 1)
            dve.wait_ge(s_par, 64)
            nc.vector.tensor_scalar(qg[:], col("q_g"), HEAD_DIM ** -0.5, None, ALU.mult).then_inc(s_set, 1)

            def w_low(f):
                dve.wait_ge(s_whi, f + 1)
                nc.vector.tensor_tensor(win_lo[:, f].rearrange("p k n -> p (k n)"), w_raw[f % 4],
                                        win_hi[:, f].rearrange("p k n -> p (k n)").bitcast(F32), ALU.subtract) \
                  .then_inc(s_wlo, 1)

            def norm_h(t):
                dve.wait_ge(s_nrt, t + 1)
                nc.vector.reciprocal(n_inv[:], n_rms[:]).then_inc(s_nin, 1)
                dve.wait_ge(s_nin, t + 1)
                for k in range(KT):
                    nc.vector.scalar_tensor_tensor(hb[:, k, :], xs[t % 2][:, k, :], col("g1", k), n_inv[:],
                                                   ALU.mult, ALU.mult).then_inc(s_hf, 1)

            def qk_copy(t, m):
                M = NORMED * t + m
                dve.wait_ge(s_pj, PROJ * t + F_K + m + 1)
                if M >= 2:
                    dve.wait_ge(s_qn, M - 1)
                dve.wait_ge(s_qs, M + 1)
                nc.vector.tensor_copy(q_raw[M % 2][:], bank[(PROJ * t + F_K + m) % PROJ_BANKS][:, 0:TA]) \
                  .then_inc(s_qr, 1)

            def qk_norm(t, m):
                M = NORMED * t + m
                dve.wait_ge(s_qrt, M + 1)
                nc.vector.reciprocal(q_inv[M % 2][:], q_rms[M % 2][:]).then_inc(s_qin, 1)
                dve.wait_ge(s_qin, M + 1)
                if M >= 2:
                    dve.wait_ge(s_qst[M % 2], 16 * (M // 2))
                dve.wait_ge(s_qr, M + 1)
                nc.vector.scalar_tensor_tensor(q_nrm[M % 2][:], q_raw[M % 2][:], col("k_g") if m == 0 else qg[:, 0:1],
                                               q_inv[M % 2][:], ALU.mult, ALU.mult).then_inc(s_qn, 1)

            w_low(0)
            norm_h(0)
            for f in range(1, PROJ):
                w_low(f)
            slots = 10
            for t in range(STEPS):
                if t > 0:
                    qk_norm(t - 1, NORMED - 1)
                conv_slot(t, 0, slots)
                for j in range(CT):
                    g = CT * t + j
                    dve.wait_ge(s_sig, g + 1)
                    if g >= 2:
                        dve.wait_ge(s_ust[j % 2], 16 * (g // 2))
                    nc.vector.tensor_tensor(ub[j % 2][:], bank[(PROJ * t + 2 * j) % PROJ_BANKS][:, 0:TA],
                                            sig[j % 2][:], ALU.mult).then_inc(s_u, 1)
                    conv_slot(t, 1 + j, slots)
                if t + 1 < STEPS:
                    norm_h(t + 1)
                conv_slot(t, 5, slots)
                qk_copy(t, 0)
                for m in range(1, NORMED):
                    qk_copy(t, m)
                    qk_norm(t, m - 1)
                    conv_slot(t, 5 + m, slots)
            qk_norm(STEPS - 1, NORMED - 1)

            def ln_centre(c):
                dve.wait_ge(s_l["mean"], c + 1)
                dve.wait_ge(s_cc, 16 * (c + 1))
                nc.vector.tensor_tensor(cc[:], cc[:], st_a[:].rearrange("p (o n) -> p o n", o=1)
                                        .to_broadcast([P, CT, TB]), ALU.subtract).then_inc(s_l["centred"], 1)

            def ln_scale(c):
                dve.wait_ge(s_l["root"], c + 1)
                nc.vector.reciprocal(st_b[:], st_a[:]).then_inc(s_l["inverse"], 1)
                dve.wait_ge(s_l["inverse"], c + 1)
                dve.wait_ge(s_lsq, CT * (c + 1))
                nc.vector.tensor_tensor(cc[:], cc[:], st_b[:].rearrange("p (o n) -> p o n", o=1)
                                        .to_broadcast([P, CT, TB]), ALU.mult).then_inc(s_l["scaled"], 1)

            def add_bias(U):
                c, u = divmod(U, UNITS)
                n, g = divmod(u, KV_HEADS)
                ks = kts(c, n)
                cols = slice(P * ks[0], P * (ks[-1] + 1))
                if U >= 2:
                    dve.wait_ge(s_t, t_seq[U - 1, kts(*divmod_block(U - 1))[0]])
                if U == 0:
                    dve.wait_ge(s_bias, 16)
                for t in range(GROUP):
                    dve.wait_ge(s_qk, GROUP * U + t + 1)
                    nc.vector.tensor_tensor_reduce(out=S[U % 2][:, t, cols], in0=bank[t][:, cols],
                                                   in1=bias[:, GROUP * g + t, cols], scale=1.0, scalar=NEG,
                                                   op0=ALU.add, op1=ALU.max, accum_out=mx[U % 2][:, t:t + 1]) \
                      .then_inc(s_sb, 1)
                sink = par[:, PARAM_AT["sink"] + GROUP * g:PARAM_AT["sink"] + GROUP * (g + 1)]
                dve.wait_ge(s_sb, GROUP * (U + 1))
                nc.vector.tensor_tensor(m4[U % 2][:], mx[U % 2][:], sink, ALU.max).then_inc(s_m4, 1)
                dve.wait_ge(s_m4, U + 1)
                nc.vector.tensor_scalar(nm4[U % 2][:], m4[U % 2][:], -1.0, None, ALU.mult).then_inc(s_nm, 1)
                nc.vector.tensor_tensor(es4[U % 2][:], sink, m4[U % 2][:], ALU.subtract).then_inc(s_es, 1)

            def normalise(U):
                c, u = divmod(U, UNITS)
                ks = kts(c, u // KV_HEADS)
                dve.wait_ge(s_ex, GROUP * (U + 1))
                dve.wait_ge(s_ee, U + 1)
                nc.vector.tensor_tensor(dn4[U % 2][:], rs4[U % 2][:], ee4[U % 2][:], ALU.add).then_inc(s_dn, 1)
                dve.wait_ge(s_dn, U + 1)
                nc.vector.reciprocal(ri4[U % 2][:], dn4[U % 2][:]).then_inc(s_ri, 1)
                dve.wait_ge(s_ri, U + 1)
                for t in range(GROUP):
                    p_ = S[U % 2][:, t, P * ks[0]:P * (ks[-1] + 1)]
                    nc.vector.tensor_scalar(p_, p_, ri4[U % 2][:, t:t + 1], None, ALU.mult).then_inc(s_p, 1)

            def divmod_block(U):
                c, u = divmod(U, UNITS)
                return c, u // KV_HEADS

            def copy_t(U):
                c, n = divmod_block(U)
                kt = kts(c, n)[-1]
                dve.wait_ge(s_t, t_seq[U, kt] + 1)
                if U >= 2:
                    dve.wait_ge(s_pv, U - 1)
                nc.vector.tensor_copy(PT[U % 2][:, kt, :], bank[4 + t_seq[U, kt] % 2][:]).then_inc(s_tv, 1)

            def attn_low(U):
                c, u = divmod(U, UNITS)
                n, g = divmod(u, KV_HEADS)
                rows = slice(HEAD_DIM * g, HEAD_DIM * (g + 1))
                dve.wait_ge(s_ahi, U + 1)
                nc.vector.tensor_tensor(cat_lo[rows, 0:AT, P * n:P * (n + 1)],
                                        bank[7][rows, :].rearrange("p (t q) -> p t q", t=AT),
                                        cat_hi[rows, 0:AT, P * n:P * (n + 1)].bitcast(F32), ALU.subtract) \
                  .then_inc(s_alo, 1)

            ln_centre(0)
            ln_scale(0)
            for o in range(KT):
                dve.wait_ge(s_wohi, o + 1)
                nc.vector.tensor_tensor(wo_lo[:, o].rearrange("p k n -> p (k n)"), wo_raw[o % 2],
                                        wo_hi[:, o].rearrange("p k n -> p (k n)").bitcast(F32), ALU.subtract) \
                  .then_inc(s_wolo, 1)
            dve.wait_ge(s_wolo, KT)
            add_bias(0)
            for c in range(CHUNKS):
                for u in range(UNITS):
                    U = UNITS * c + u
                    normalise(U)
                    if u + 1 < UNITS:
                        add_bias(U + 1)
                    if u > 0:
                        attn_low(U - 1)
                    copy_t(U)
                    if c + 1 < CHUNKS:
                        if u == 2:
                            ln_centre(c + 1)
                        if u == 5:
                            ln_scale(c + 1)
                attn_low(UNITS * c + UNITS - 1)
                for o in range(KT):
                    n = KT * c + o
                    dve.wait_ge(s_wo, n + 1)
                    if o == 0:
                        dve.wait_ge(s_xb, 16 * (c + 1))
                    nc.vector.tensor_tensor(xb[:, o, :], bank[o % 4][:], xb[:, o, :], ALU.add).then_inc(s_x2, 1)
                    pair = STEPS - CONV_LAG + c
                    if pair < PAIRS:
                        lo, hi = PAIR_OPS * o // KT, PAIR_OPS * (o + 1) // KT
                        conv_ops(PAIR_OPS * pair + lo, hi - lo)
                if c + 1 < CHUNKS:
                    add_bias(UNITS * (c + 1))
                dve.wait_ge(s_n2r, c + 1)
                nc.vector.reciprocal(n2_inv[:], n2_rms[:]).then_inc(s_n2i, 1)
                dve.wait_ge(s_n2i, c + 1)
                for k in range(KT):
                    n = KT * c + k
                    if n >= 2:
                        dve.wait_ge(s_h2st[k % 2], 16 * (n // 2))
                    nc.vector.scalar_tensor_tensor(h2b[k % 2][:], xb[:, k, :], col("g2", k), n2_inv[:],
                                                   ALU.mult, ALU.mult).then_inc(s_h2, 1)

            dve.sem_inc(s_c3, 2)
            dve.sem_inc(s_m, 2)
            dve.sem_inc(s_mlo, 2)
            for w in range(WINDOWS):
                base = TILES_W * w
                with dve.Fori(0, FT // 2) as i:
                    for s in range(2):
                        J = FT * w + 2 * i + s
                        taps = [ffn_w_ap[:, bass.ds((2 * i + s) * FFN_TAPS + r, 1)] for r in range(FFN_TAPS)]
                        b_ = par[:, bass.ds(2 * i + s + PARAM_AT["ffn_b"], 1)]
                        dve.wait_ge(s_gb, J + 3)
                        dve.wait_ge(s_m, J + 1)
                        nc.vector.tensor_scalar(cv[s][:], gb[s][:, 0:TC], taps[0], b_, ALU.mult, ALU.add) \
                          .then_inc(s_c1, 1)
                        dve.wait_ge(s_c1, J + 1)
                        nc.vector.scalar_tensor_tensor(cv[s][:], gb[s][:, 1:TC + 1], taps[1], cv[s][:],
                                                       ALU.mult, ALU.add).then_inc(s_c2, 1)
                        dve.wait_ge(s_c2, J + 1)
                        nc.vector.scalar_tensor_tensor(cv[s][:], gb[s][:, 2:TC + 2], taps[2], cv[s][:],
                                                       ALU.mult, ALU.add).then_inc(s_c3, 1)
                        dve.wait_ge(s_sl, J + 1)
                        dve.wait_ge(s_used, RING + base + 4 * i + 2 * s + 2)
                        dve.wait_ge(s_mlo, J + 1)
                        nc.vector.tensor_tensor(mb[s][:], bank[2 + s][:, 0:TC], cv[s][:], ALU.mult).then_inc(s_m, 1)
                        dve.wait_ge(s_mhi, J + 1)
                        nc.vector.tensor_tensor(mid_lo[:, bass.ds((2 * i + s) * TC, TC)], mb[s][:],
                                                mid_hi[:, bass.ds((2 * i + s) * TC, TC)].bitcast(F32),
                                                ALU.subtract).then_inc(s_mlo, 1)
                for o in range(KT):
                    n = KT * w + o
                    dve.wait_ge(s_used, RING + base + TILES_F + DOWN_PIECES * (o + 1))
                    dve.wait_ge(s_x2w[o % 2], 16 * (n // 2 + 1))
                    if n >= 2:
                        dve.wait_ge(s_yst[o % 2], 16 * (n // 2))
                    nc.vector.tensor_tensor(yb[o % 2][:], bank[4 + o % 2][:, 0:TC], x2w[o % 2][:], ALU.add) \
                      .then_inc(s_y, 1)

        @block.tensor
        def _(pe):
            def norm_sum(t):
                pe.wait_ge(s_xsq, t + 1)
                if t > 0:
                    pe.wait_ge(s_nrt, t)
                for k in range(KT):
                    mm = nc.tensor.matmul(bank[7][:, 0:TA], ones[:], hb[:, k, :], start=(k == 0), stop=(k == KT - 1))
                mm.then_inc(s_nst, 1)

            def bank_free(n):
                t, f = divmod(n, PROJ)
                if f < F_V and f % 2 == 0:
                    pe.wait_ge(s_u, CT * t + f // 2 + 1)
                elif f < F_V:
                    pe.wait_ge(s_sig, CT * t + f // 2 + 1)
                elif f == F_V:
                    pe.wait_ge(s_v, t + 1)
                else:
                    pe.wait_ge(s_qr, NORMED * t + f - F_K + 1)

            def project(t, f):
                n = PROJ * t + f
                if n >= PROJ_BANKS:
                    bank_free(n - PROJ_BANKS)
                if t == 0:
                    pe.wait_ge(s_wlo, f + 1)
                if f == 0:
                    pe.wait_ge(s_hlo, t + 1)
                out = bank[n % PROJ_BANKS]
                hi, lo = h_hi[t % 2], h_lo[t % 2]
                if f == F_V:
                    for b_ in range(TA // P):
                        toks = slice(P * b_, P * (b_ + 1))
                        i = 0
                        for k in range(KT):
                            for l, r in ((hi, win_hi), (hi, win_lo), (lo, win_hi)):
                                mm = nc.tensor.matmul(out[:, KV_W * b_:KV_W * (b_ + 1)], l[:, k, toks], r[:, f, k, :],
                                                      start=(i == 0), stop=(i == 3 * KT - 1))
                                i += 1
                else:
                    i = 0
                    for k in range(KT):
                        for l, r in ((win_hi, hi), (win_hi, lo), (win_lo, hi)):
                            mm = nc.tensor.matmul(out[:, 0:TA], l[:, f, k, :], r[:, k, :],
                                                  start=(i == 0), stop=(i == 3 * KT - 1))
                            i += 1
                mm.then_inc(s_pj, 1)

            def qk_sum(t, m):
                M = NORMED * t + m
                pe.wait_ge(s_qs, M + 1)
                if M >= 2:
                    pe.wait_ge(s_qrt, M - 1)
                nc.tensor.matmul(bank[4 + M % 2][:, 0:TA], halves[:], q_sq[M % 2][:], start=True, stop=True) \
                  .then_inc(s_qss, 1)

            pe.wait_ge(s_par, 64)
            norm_sum(0)
            for t in range(STEPS):
                for f in range(PROJ):
                    project(t, f)
                    if f == 0 and t > 0:
                        qk_sum(t - 1, NORMED - 1)
                    if f == F_V - 1 and t + 1 < STEPS:
                        norm_sum(t + 1)
                    if f > F_K:
                        qk_sum(t, f - F_K - 1)
            qk_sum(STEPS - 1, NORMED - 1)

            def ln_sum(c):
                pe.wait_ge(s_cc, 16 * (c + 1))
                if c > 0:
                    pe.wait_ge(s_n2r, c - 1) if c > 1 else None
                for j in range(CT):
                    mm = nc.tensor.matmul(bank[6][:], ones[:], cc[:, j, :], start=(j == 0), stop=(j == CT - 1))
                mm.then_inc(s_l["sum"], 1)

            def ln_var(c):
                for j in range(CT):
                    pe.wait_ge(s_lsq, CT * c + j + 1)
                    nc.tensor.matmul(bank[6][:], ones[:], sq[j % 2][:], start=(j == 0), stop=(j == CT - 1)) \
                      .then_inc(s_l["var"], 1)

            def scores(U):
                c, u = divmod(U, UNITS)
                n, g = divmod(u, KV_HEADS)
                ks = kts(c, n)
                rows = slice(HEAD_DIM * g, HEAD_DIM * (g + 1))
                if u == 0:
                    pe.wait_ge(s_qkv, 48 * (c + 1))
                    if c > 0:
                        pe.wait_ge(s_x2, KT * c)
                for t in range(GROUP):
                    if U > 0:
                        pe.wait_ge(s_sb, GROUP * (U - 1) + t + 1)
                    nc.tensor.matmul(bank[t][:, P * ks[0]:P * (ks[-1] + 1)], qw[rows, t, P * n:P * (n + 1)],
                                     kw[rows, P * (n + ks[0]):P * (n + ks[-1] + 1)], start=True, stop=True) \
                      .then_inc(s_qk, 1)

            def transposes(U):
                c, u = divmod(U, UNITS)
                for kt in kts(c, u // KV_HEADS):
                    i = t_seq[U, kt]
                    if i >= 2:
                        wait_copied(pe, *t_list[i - 2])
                    for t in range(GROUP):
                        pe.wait_ge(s_p, GROUP * U + t + 1)
                        mm = nc.tensor.transpose(bank[4 + i % 2][:, P * t:P * (t + 1)],
                                                 S[U % 2][:, t, P * kt:P * (kt + 1)], ident[:])
                    mm.then_inc(s_t, 1)

            def values(U):
                c, u = divmod(U, UNITS)
                n = u // KV_HEADS
                ks = kts(c, n)
                if U > 0:
                    pe.wait_ge(s_alo, U)
                for kt in ks:
                    wait_copied(pe, U, kt)
                    mm = nc.tensor.matmul(bank[7][:], vw[:, n + kt, :], PT[U % 2][:, kt, :],
                                          start=(kt == ks[0]), stop=(kt == ks[-1]))
                mm.then_inc(s_pv, 1)

            def norm2_term(c, o):
                pe.wait_ge(s_x2q, KT * c + o + 1)
                if o == 0 and c + 1 < CHUNKS:
                    pe.wait_ge(s_l["root"], c + 2)
                nc.tensor.matmul(bank[6][:], ones[:], sq[o % 2][:], start=(o == 0), stop=(o == KT - 1)) \
                  .then_inc(s_n2m, 1)

            ln_sum(0)
            pe.wait_ge(s_l["mean"], 1)
            ln_var(0)
            scores(0)
            for c in range(CHUNKS):
                for u in range(UNITS):
                    U = UNITS * c + u
                    if u + 1 < UNITS:
                        scores(U + 1)
                    if u > 0:
                        values(U - 1)
                    transposes(U)
                    if c + 1 < CHUNKS:
                        if u == 1:
                            if c > 0:
                                pe.wait_ge(s_n2r, c)
                            ln_sum(c + 1)
                        if u == 3:
                            pe.wait_ge(s_l["mean"], c + 2)
                            ln_var(c + 1)
                values(UNITS * c + UNITS - 1)
                for o in range(KT):
                    n = KT * c + o
                    if c == 0:
                        pe.wait_ge(s_wolo, o + 1)
                    if o < 4:
                        pe.wait_ge(s_sb, GROUP * UNITS * (c + 1))
                    else:
                        pe.wait_ge(s_x2, n - 3)
                    if o == 0:
                        pe.wait_ge(s_l["lo"], c + 1)
                    i = 0
                    for k in (*range(AT, KT), *range(AT)):
                        if k == 0 and o == 0:
                            pe.wait_ge(s_alo, UNITS * (c + 1))
                        for l, r in ((wo_hi, cat_hi), (wo_hi, cat_lo), (wo_lo, cat_hi)):
                            mm = nc.tensor.matmul(bank[o % 4][:], l[:, o, k, :], r[:, k, :],
                                                  start=(i == 0), stop=(i == 3 * KT - 1))
                            i += 1
                    mm.then_inc(s_wo, 1)
                    if o > 0:
                        norm2_term(c, o - 1)
                if c + 1 < CHUNKS:
                    scores(UNITS * (c + 1))
                norm2_term(c, KT - 1)

            pe.sem_inc(s_used, RING)
            passes = ((whi, hw_hi), (whi, hw_lo), (wlo, hw_hi))
            for w in range(WINDOWS):
                base = TILES_W * w
                pe.wait_ge(s_hwlo, w + 1)
                if w == 0:
                    pe.wait_ge(s_n2r, CHUNKS)
                with pe.Fori(0, FT // 2) as i:
                    for s in range(2):
                        J = FT * w + 2 * i + s
                        pe.wait_ge(s_flo, base + 4 * i + 2 * s + 1 + RING)
                        pe.wait_ge(s_gb, J + 1)
                        x_ = 0
                        for k in range(KT):
                            for l, r in passes:
                                mm = nc.tensor.matmul(bank[s][:, 0:TH], l[2 * s][:, k, :], r[:, k, :],
                                                      start=(x_ == 0), stop=(x_ == 3 * KT - 1))
                                x_ += 1
                        mm.then_inc(s_used, 1)
                        pe.wait_ge(s_flo, base + 4 * i + 2 * s + 2 + RING)
                        pe.wait_ge(s_m, J + 1)
                        x_ = 0
                        for k in range(KT):
                            for l, r in passes:
                                mm = nc.tensor.matmul(bank[2 + s][:, 0:TC], l[2 * s + 1][:, k, :], r[:, k, 1:TC + 1],
                                                      start=(x_ == 0), stop=(x_ == 3 * KT - 1))
                                x_ += 1
                        mm.then_inc(s_used, 1)
                pe.wait_ge(s_mlo, FT * (w + 1) + 2)
                for o in range(KT):
                    n = KT * w + o
                    if n >= 2:
                        pe.wait_ge(s_y, n - 1)
                    x_ = 0
                    for s in range(DOWN_PIECES):
                        tile = TILES_F + DOWN_PIECES * o + s
                        slot = tile % RING
                        pe.wait_ge(s_flo, base + tile + 1 + RING)
                        ks = range(W_PIECE * s, min(W_PIECE * (s + 1), FT))
                        for k in ks:
                            for l, r in ((whi, mid_hi), (whi, mid_lo), (wlo, mid_hi)):
                                mm = nc.tensor.matmul(bank[4 + o % 2][:, 0:TC], l[slot][:, k - W_PIECE * s, :],
                                                      r[:, TC * k:TC * (k + 1)],
                                                      start=(x_ == 0), stop=(x_ == 3 * FT - 1))
                                x_ += 1
                        mm.then_inc(s_used, 1)


def constants():
    ones = np.ones((P, P), np.float32)
    halves = np.kron(np.eye(2, dtype=np.float32), np.ones((HEAD_DIM, HEAD_DIM), np.float32))
    dist = np.abs(np.arange(P)[:, None] + P - np.arange(BAND)[None, :]).astype(np.float32)
    slopes = np.array([2.0 ** (-8.0 * (h + 1) / HEADS) for h in range(HEADS)], np.float32)
    bias = np.where(dist[:, None, :] <= WINDOW, -slopes[None, :, None] * dist[:, None, :], np.float32(NEG))
    return np.concatenate([ones, halves, np.eye(P, dtype=np.float32), bias.reshape(P, -1).astype(np.float32)], 1)


def weight_tiles(w):
    k, n = w.shape
    return w.reshape(k // P, P, n // P, P).transpose(2, 1, 0, 3)


def by_partition(v):
    v = v.reshape(*v.shape[:-1], v.shape[-1] // P, P)
    return np.moveaxis(np.moveaxis(v, -1, 0), -1, 1).reshape(P, -1)


def kernel(**inputs):
    import concourse.bacc as bacc
    from concourse.bass_utils import run_bass_kernel_spmd

    i = {k: np.asarray(v) for k, v in inputs.items()}
    x = np.concatenate([i["x_prompt"][0], i["x_sample"][0]], 0).T.reshape(KT, P, TOKENS).transpose(1, 0, 2)
    w_in = i["w_in"][0]
    q, k, v, glu_a, glu_g = np.split(w_in, [ATTN_W, ATTN_W + KV_W, ATTN_W + 2 * KV_W, ATTN_W + 2 * KV_W + CONV_W], 1)
    q = q.reshape(D_MODEL, KV_HEADS, GROUP, HEAD_DIM).transpose(0, 2, 1, 3).reshape(D_MODEL, ATTN_W)
    glu = np.stack([weight_tiles(glu_a), weight_tiles(glu_g)], 1).reshape(2 * CT, P, KT, P)
    w_in_t = np.concatenate([glu, weight_tiles(v), weight_tiles(k), weight_tiles(q)], 0)
    w_out = i["w_out"][0]
    attn_rows = w_out[:ATTN_W].reshape(KV_HEADS, GROUP, HEAD_DIM, D_MODEL).transpose(1, 0, 2, 3)
    w_out_t = weight_tiles(np.concatenate([attn_rows.reshape(ATTN_W, D_MODEL), w_out[ATTN_W:]], 0))
    w_ffn = np.stack([weight_tiles(i["ffn_w_gate"][0]), weight_tiles(i["ffn_w_up"][0])], 1)
    w_ffn = w_ffn.reshape(TILES_F, P, KT, P)
    down = weight_tiles(i["ffn_w_down"][0])
    down = np.concatenate([down, np.zeros((KT, P, DOWN_PIECES * W_PIECE - FT, P), down.dtype)], 2)
    w_down = down.reshape(KT, P, DOWN_PIECES, W_PIECE, P).transpose(0, 2, 1, 3, 4)
    packed = {
        "g1": by_partition(i["norm1_g"][0]), "g2": by_partition(i["norm2_g"][0]),
        "conv_w": by_partition(i["conv_dw_w"][0]),
        "conv_b": by_partition(i["conv_dw_b"][0]),
        "ln_g": by_partition(i["conv_ln_g"][0]), "ln_b": by_partition(i["conv_ln_b"][0]),
        "ffn_w": by_partition(i["ffn_dw_w"][0]),
        "ffn_b": by_partition(i["ffn_dw_b"][0]),
        "q_g": np.tile(i["q_norm_g"][0], 2)[:, None], "k_g": np.tile(i["k_norm_g"][0], 2)[:, None],
        "sink": np.tile(i["attn_sink"][0], (P, 1)),
    }
    params = np.concatenate([packed[name] for name, _ in PARAM_SPLIT], 1)
    arrays = {"x_t": x, "w_in_t": w_in_t, "w_out_t": w_out_t, "w_ffn_t": w_ffn, "w_down_t": w_down,
              "params": params, "consts": constants()}
    arrays = {name: np.ascontiguousarray(a) for name, a in arrays.items()}

    nc = bacc.Bacc("TRN2", target_bir_lowering=False, num_devices=1)
    args = [nc.dram_tensor(name, a.shape, mybir.dt.from_np(a.dtype), kind="ExternalInput").ap()
            for name, a in arrays.items()]
    y = nc.dram_tensor("y_t", (KT, P, OUT_COLS), F32, kind="ExternalOutput").ap()
    encoder_layer(nc, *args, y)
    got = run_bass_kernel_spmd(nc, [arrays], core_ids=[0]).results[0]["y_t"]
    got = np.asarray(got).reshape(D_MODEL, OUT_COLS).T
    y_prompt = np.ascontiguousarray(got[:PROMPT])[None]
    y_sample = np.ascontiguousarray(got[PROMPT + 1:PROMPT + 1 + SAMPLE])[None]
    return y_prompt, y_sample
```

```python
from contextlib import ExitStack

import numpy as np
import concourse.bass as bass
from concourse import mybir

F32 = mybir.dt.float32
F32R = mybir.dt.float32r
ALU = mybir.AluOpType
ACT = mybir.ActivationFunctionType

P = 128
D_MODEL = 1024
PROMPT, SAMPLE = 512, 2048
TOKENS = PROMPT + SAMPLE
HEADS, KV_HEADS, HEAD_DIM = 8, 2, 64
GROUP = HEADS // KV_HEADS
ATTN_W = HEADS * HEAD_DIM
KV_W = KV_HEADS * HEAD_DIM
CONV_W = D_MODEL - ATTN_W
TAPS = 31
HALO = TAPS // 2
WINDOW = 128
D_FF = 2816
FFN_TAPS = 3

KT = D_MODEL // P
CT = CONV_W // P
FT = D_FF // P
AT = ATTN_W // P

TA = 256
STEPS = TOKENS // TA
PROJ = 2 * CT + 2 + AT
NORMED = 1 + AT
F_V, F_G = NORMED, NORMED + 1
SLOTS = 5
NORM_ROWS = NORMED * KV_HEADS

C_PICK = 2 * P
C_SPREAD = C_PICK + 2 * NORM_ROWS - KV_HEADS
C_BIAS = C_SPREAD + NORMED * P

TB = 512
CHUNKS = TOKENS // TB
BLOCKS = TB // P
UNITS = BLOCKS * KV_HEADS
BAND = 3 * P

CONV_UNITS = CHUNKS * CT
PAIR_OPS = 2 * TAPS
CONV_OPS = CONV_UNITS * TAPS
SQUARE_AFTER = (4, 5, 7, 8, 10)
GLU_AFTER = (0,)
CONV_A = (0, 0, 39, 39, 40, 50, 48, 47, 47, 43)
CONV_B_UNITS = ((5, 5, 5, 5, 5, 5, 5, 5), (8, 7, 5, 5, 5, 5, 6, 7), (8, 7, 6, 6, 6, 6, 7, 8),
                (8, 8, 7, 7, 6, 6, 6, 6), (0,) * 8)
CONV_B_OUT = (3, 3, 5, 1, 6, 0, 4, 3)
CONV_B_CHUNKS = 3
OUT_BANKS = (6, 4, 5, 7, 4, 5, 7, 6)
PROMPT_U = PROMPT + 2 * HALO
U_COLS = PROMPT_U + SAMPLE + 2 * HALO

TC = 428
WINDOWS = 6
OUT_COLS = TC * WINDOWS
PAD_COLS = OUT_COLS + 2
PAD_SPANS = ((0, 1), (1 + PROMPT, 1), (2 + TOKENS, PAD_COLS - TOKENS - 2))
ZERO_STORES = 4 + 2 * len(PAD_SPANS)
TH = TC + 2
W_PIECE = 8
DOWN_PIECES = -(-FT // W_PIECE)
TILES_F = 2 * FT
TILES_D = KT * DOWN_PIECES
TILES_W = TILES_F + TILES_D
RING = 4

NEG = -1e30

PARAM_SPLIT = [("g1", KT), ("g2", KT), ("conv_w", CT * TAPS), ("conv_b", CT), ("ln_g", CT), ("ln_b", CT),
               ("ffn_w", FT * FFN_TAPS), ("ffn_b", FT), ("q_g", 1), ("k_g", 1), ("sink", HEADS)]
PARAM_AT = {}
PARAM_COLS = 0
for _name, _n in PARAM_SPLIT:
    PARAM_AT[_name] = PARAM_COLS
    PARAM_COLS += _n


def padded(c):
    return 1 + TB * c + (1 if TB * c >= PROMPT else 0)


def u_window(c):
    return 0 if c == 0 else PROMPT_U + TB * (c - 1)


def u_column(t):
    return HALO + TA * t if TA * t < PROMPT else PROMPT_U + HALO + TA * t - PROMPT


def unit_last_op(unit):
    return PAIR_OPS * (unit // 2) + PAIR_OPS - 2 + unit % 2


def encoder_layer(nc, x, x_tok, w_in, w_out, w_ffn, w_down, params, consts, y):
    with ExitStack() as ctx:
        def dram(name, shape):
            return nc.dram_tensor(name, shape, F32, kind="Internal").ap()

        q_d = dram("q_scratch", (AT, P, TOKENS))
        k_d = dram("k_scratch", (P, TOKENS))
        v_d = dram("v_scratch", (TOKENS // P, P, KV_W))
        u_d = dram("u_scratch", (CT, P, U_COLS))
        c_d = dram("conv_scratch", (CT, P, TOKENS))
        x2_d = dram("x2_scratch", (KT, P, PAD_COLS))
        h2_d = dram("h2_scratch", (KT, P, PAD_COLS))

        def sb(name, shape, dt=F32):
            return ctx.enter_context(nc.sbuf_tensor(name, shape, dt))

        def pair(name, shape, dt=F32):
            return [sb(f"{name}{i}", shape, dt) for i in range(2)]

        def sem(name):
            return ctx.enter_context(nc.semaphore(name))

        bank = [ctx.enter_context(nc.psum_tensor(f"bank{i}", [P, 512], F32)) for i in range(8)]

        par = sb("par", [P, PARAM_COLS])
        ones = sb("ones", [P, P])
        pick = sb("pick", [P, 2 * NORM_ROWS - KV_HEADS])
        ident = sb("ident", [P, P])
        eps = sb("eps", [P, 2])
        qg = sb("qg", [P, 1])
        t_ss = pair("t_ss", [P, TA // P])
        t_rt = pair("t_rt", [P, TA // P])
        t_rs = pair("t_rs", [P, TA // P])
        mx, m4, nm4, es4, rs4, ee4, dn4, ri4 = (pair(name, [P, GROUP]) for name in (
            "row_max", "shift", "neg_shift", "sink_shifted", "row_sum", "sink_exp", "denom", "inv_denom"))

        base0 = -(-nc.sbuf_base // 32) * 32
        tile_b = 4 * P * KT
        R_QK = KT * tile_b
        R_LO = PROJ * tile_b
        R_LO2 = R_LO + KT * tile_b
        R_H1 = 2 * PROJ * tile_b
        R_SM = R_H1 + 2 * 4 * KT * TA
        R_QN = R_SM + 8 * 4 * TA + 4 * NORMED * P
        R_CV = R_QN + NORMED * 4 * TA
        conv_b = -(-4 * (TB + 2 * HALO) // 32) * 32 + 4 * TB
        R_PR = R_CV + 4 * conv_b
        place_end = R_PR + 43 * 1024

        def at(offset, name, shape, dt=F32):
            size = 4 * int(np.prod(shape[1:]))
            assert offset + size <= place_end, name
            return nc.alloc_sbuf_tensor_at(name, shape, dt, offset=base0 + offset), offset + -(-size // 32) * 32

        def run(offset, *specs):
            got = []
            for name, shape, dt in specs:
                t, offset = at(offset, name, shape, dt)
                got.append(t)
            return got

        conv = run(R_CV, *[(f"conv_win{i}", [P, TB + 2 * HALO], F32) for i in range(4)],
                   *[(f"conv_acc{i}", [P, TB], F32) for i in range(4)])
        conv_win, conv_acc = conv[:4], conv[4:]
        zeros = conv_acc[3][:, 0:max(CT * HALO, KT * PAD_SPANS[-1][1])]

        win_hi, = run(0, ("win_hi", [P, PROJ, KT, P], F32R))
        win_lo, = run(R_LO, ("win_lo", [P, PROJ, KT, P], F32R))
        h1 = run(R_H1, ("h_hi1", [P, KT, TA], F32R), ("h_lo1", [P, KT, TA], F32R))
        w_raw = [t[:] for t in run(R_H1, *[(f"w_raw{i}", [P, KT * P], F32) for i in range(4)])]
        sm = run(R_SM, *[(n, [P, TA], F32) for n in ("sig0", "sig1", "ub0", "ub1", "q_sq0", "q_sq1", "q_inv", "vb")],
                 ("spread", [P, NORMED * P], F32), *[(f"qk{m}", [P, TA], F32) for m in range(NORMED)])
        sig, ub, q_sq, q_inv, vb, spread, qk = sm[0:2], sm[2:4], sm[4:6], *sm[6:9], sm[9:]
        q_root, v_raw = sig[0], sig[1]
        *h0, hb, xs0, xs1 = run(R_PR, ("h_hi0", [P, KT, TA], F32R), ("h_lo0", [P, KT, TA], F32R),
                                ("hb", [P, KT, TA], F32), ("xs0", [P, KT, TA], F32), ("xs1", [P, KT, TA], F32))
        xt = hb[:].rearrange("p k n -> p (k n)").rearrange("p (b d) -> p b d", b=TA // P)
        h_hi, h_lo, xs = [h0[0], h1[0]], [h0[1], h1[1]], [xs0, xs1]

        wo_hi, = run(0, ("wo_hi", [P, KT, KT, P], F32R))
        wo_lo, = run(R_LO, ("wo_lo", [P, KT, KT, P], F32R))
        s0, s1, pt0, pt1 = run(R_QK, ("S0", [P, GROUP, BAND], F32), ("S1", [P, GROUP, BAND], F32),
                               ("PT0", [P, 3, TB], F32), ("PT1", [P, 3, TB], F32))
        S, PT = [s0, s1], [pt0, pt1]
        xb, cat_hi, cat_lo, tmp1 = run(R_LO2, ("xb", [P, KT, TB], F32), ("cat_hi", [P, KT, TB], F32R),
                                       ("cat_lo", [P, KT, TB], F32R), ("tmp1", [P, TB], F32))
        qw, kw, bias, cc, ln_acc, wo_r0, wo_r1, ln_st = run(
            R_PR, ("qw", [P, AT, TB], F32), ("kw", [P, TB + 2 * P], F32), ("bias", [P, HEADS, BAND], F32),
            ("cc", [P, CT, TB], F32), ("ln_acc", [P, TB], F32), ("wo_r0", [P, KT * P], F32), ("wo_r1", [P, KT * P], F32),
            ("ln_st", [P, TB], F32))
        vw, tmp0 = run(R_QN, ("vw", [P, BLOCKS + 2, KV_W], F32), ("tmp0", [P, TB], F32))
        wo_raw = [wo_r0, wo_r1]
        tmp = [tmp0, tmp1]
        r_st = R_PR + 4 * (AT * TB + TB + 2 * P + HEADS * BAND + CT * TB + TB)
        sq0, sq1, n2_acc, n2_rs = run(r_st, *[(n, [P, TB], F32) for n in ("sq0", "sq1", "n2_acc", "n2_rs")])
        sq = [sq0, sq1]

        hw_raw, hw_hi, hw_lo, wr0, wr1 = run(
            R_CV, ("hw_raw", [P, KT, TH], F32), ("hw_hi", [P, KT, TH], F32R), ("hw_lo", [P, KT, TH], F32R),
            ("wraw0", [P, W_PIECE, P], F32), ("wraw1", [P, W_PIECE, P], F32))
        wsp = run(R_QK, *[(f"w{part}{i}", [P, W_PIECE, P], F32R) for i in range(RING - 1) for part in ("hi", "lo")])
        wh3, wl3, mid = run(R_LO, ("whi3", [P, W_PIECE, P], F32R), ("wlo3", [P, W_PIECE, P], F32R),
                            ("mid", [P, FT * 2 * TC], F32R))

        def mid_hi(f):
            return mid[:, bass.ds(f * (2 * TC), TC)]

        def mid_lo(f):
            return mid[:, bass.ds(f * (2 * TC) + TC, TC)]

        gb0, gb1, wr2, wr3, *rest = run(
            0, ("gb0", [P, TH], F32), ("gb1", [P, TH], F32), ("wraw2", [P, W_PIECE, P], F32),
            ("wraw3", [P, W_PIECE, P], F32),
            *[(n, [P, TC], F32) for n in ("cv0", "cv1", "mb0", "mb1", "x2w0", "x2w1", "yb0", "yb1")])
        gb, cv, mb, x2w, yb = [gb0, gb1], rest[0:2], rest[2:4], rest[4:6], rest[6:8]
        wraw, whi, wlo = [wr0, wr1, wr2, wr3], [*wsp[0::2], wh3], [*wsp[1::2], wl3]

        def col(name, i=0):
            return par[:, PARAM_AT[name] + i:PARAM_AT[name] + i + 1]

        ffn_w_ap = par[:, PARAM_AT["ffn_w"]:PARAM_AT["ffn_w"] + FT * FFN_TAPS]

        s_par = sem("params_loaded")
        s_ones = sem("ones_loaded")
        s_set = sem("constants_set")
        s_zst = sem("pads_stored")
        s_x = [sem(f"x_loaded{i}") for i in range(2)]
        s_xt = sem("x_tokens_loaded")
        s_wr = [sem(f"w_in_loaded{i}") for i in range(4)]
        s_whi = sem("w_in_hi_ready")
        s_wlo = sem("w_in_lo_ready")
        s_tsq = sem("norm1_squares_summed")
        s_trt = sem("norm1_root_ready")
        s_trs = sem("norm1_scale_ready")
        s_nst = sem("norm1_scale_spread")
        s_hf = sem("h_ready")
        s_hhi = sem("h_hi_ready")
        s_hlo = sem("h_lo_ready")
        s_pj = sem("projection_ready")
        s_sig = sem("glu_sigmoid_ready")
        s_u = sem("glu_ready")
        s_ust = [sem(f"glu_stored{i}") for i in range(2)]
        s_vr = sem("v_copied")
        s_vt = sem("v_transposed")
        s_v = sem("v_ready")
        s_vst = sem("v_stored")
        s_qc = sem("qk_copied")
        s_qs = sem("qk_squared")
        s_qss = sem("qk_sum_ready")
        s_qrt = sem("qk_root_ready")
        s_qri = sem("qk_scale_ready")
        s_qsp = sem("qk_scale_spread")
        s_qn = sem("qk_normed")
        s_qst = [sem(f"qk_stored{m}") for m in range(NORMED)]
        s_win = [sem(f"conv_window_loaded{i}") for i in range(4)]
        s_cv = sem("conv_step_done")
        s_cst = [sem(f"conv_stored{i}") for i in range(4)]

        s_bias = sem("bias_loaded")
        s_wor = [sem(f"w_out_loaded{i}") for i in range(2)]
        s_wohi = sem("w_out_hi_ready")
        s_wolo = sem("w_out_lo_ready")
        s_qkl = sem("qk_loaded")
        s_vl = sem("v_loaded")
        s_cc = sem("conv_loaded")
        s_xb = sem("residual_loaded")
        s_l = {k: sem(f"ln_{k}") for k in ("added", "sum", "mean", "centred", "squared", "sq_added", "var", "log",
                                           "scale", "scaled", "swish", "hi", "lo")}
        s_qk = sem("scores_ready")
        s_sb = sem("scores_biased")
        s_m4 = sem("max_ready")
        s_nm = sem("negmax_ready")
        s_es = sem("sink_shifted_ready")
        s_ex = sem("exp_ready")
        s_ee = sem("sink_exp_ready")
        s_dn = sem("denominator_ready")
        s_ri = sem("inverse_denominator_ready")
        s_p = sem("probs_ready")
        s_t = sem("probs_transposed")
        s_pt = sem("probsT_copied")
        s_pv = sem("attention_ready")
        s_ahi = sem("attention_hi_ready")
        s_alo = sem("attention_lo_ready")
        s_wo = sem("out_projection_ready")
        s_x2 = sem("x2_ready")
        s_x2q = sem("x2_squared")
        s_n2a = sem("norm2_added")
        s_n2m = sem("norm2_sum_ready")
        s_n2l = sem("norm2_log_ready")
        s_n2s = sem("norm2_scale_ready")
        s_h2 = sem("h2_ready")
        s_x2st = sem("x2_stored")
        s_h2st = [sem(f"h2_stored{i}") for i in range(2)]

        s_hw = sem("window_loaded")
        s_hwhi = sem("window_hi_ready")
        s_hwlo = sem("window_lo_ready")
        s_rw = [sem(f"ffn_weight_loaded{i}") for i in range(RING)]
        s_fhi = sem("ffn_weight_hi_ready")
        s_flo = sem("ffn_weight_lo_ready")
        s_used = sem("ffn_products_done")
        s_gb = sem("gate_copied")
        s_c1 = sem("ffn_tap1_done")
        s_c2 = sem("ffn_tap2_done")
        s_c3 = sem("ffn_conv_ready")
        s_sl = sem("ffn_swish_ready")
        s_m = sem("mid_ready")
        s_mhi = sem("mid_hi_ready")
        s_mlo = sem("mid_lo_ready")
        s_x2w = [sem(f"residual_window_loaded{i}") for i in range(2)]
        s_y = sem("y_ready")
        s_yst = [sem(f"y_stored{i}") for i in range(2)]

        def proj_bank(n):
            return bank[n % SLOTS][:, 0:TA]

        spread_bank = [bank[7], bank[5]]

        block = ctx.enter_context(nc.Block())

        def kts(c, n):
            first = n == 0 and c in (0, 1)
            last = n == BLOCKS - 1 and c in (0, CHUNKS - 1)
            return [k for k in range(3) if not (k == 0 and first) and not (k == 2 and last)]

        def band_blocks(c):
            return (1 if c in (0, 1) else 0), BLOCKS + 2 - (1 if c in (0, CHUNKS - 1) else 0)

        def unit_of(U):
            c, u = divmod(U, UNITS)
            n, g = divmod(u, KV_HEADS)
            return c, n, g, kts(c, n)

        t_seq = {}
        for U in range(UNITS * CHUNKS):
            for kt in unit_of(U)[3]:
                t_seq[U, kt] = len(t_seq)

        def t_end(U):
            return t_seq[U, unit_of(U)[3][-1]] + 1

        @block.sync
        def _(sp):
            def load_x(t):
                if t >= 2:
                    sp.wait_ge(s_hf, KT * (t - 1))
                sp.dma_start(xs[t % 2][:], x[:, :, TA * t:TA * (t + 1)]).then_inc(s_x[t % 2], 16)

            def load_xt(t):
                if t >= 1:
                    sp.wait_ge(s_hlo, t)
                sp.dma_start(xt, x_tok[t]).then_inc(s_xt, 16)

            def store_qk(t, m):
                M = NORMED * t + m
                sp.wait_ge(s_qn, M + 1)
                dst = k_d if m == 0 else q_d[m - 1]
                sp.dma_start(dst[:, TA * t:TA * (t + 1)], qk[m][:]).then_inc(s_qst[m], 16)

            def store_u(t, j):
                sp.wait_ge(s_u, CT * t + j + 1)
                sp.dma_start(u_d[j, :, u_column(t):u_column(t) + TA], ub[j % 2][:]).then_inc(s_ust[j % 2], 16)

            def load_qk(c):
                if c > 0:
                    sp.wait_ge(s_qk, GROUP * UNITS * c)
                else:
                    for m in range(NORMED):
                        sp.wait_ge(s_qst[m], 16 * (STEPS - 1))
                sp.dma_start(qw[:], q_d.rearrange("t p n -> p t n")[:, :, TB * c:TB * (c + 1)]).then_inc(s_qkl, 16)
                n0, n1 = band_blocks(c)
                t0 = BLOCKS * c - 1
                sp.dma_start(kw[:, P * n0:P * n1], k_d[:, P * (t0 + n0):P * (t0 + n1)]).then_inc(s_qkl, 16)

            def load_v(c):
                if c > 0:
                    sp.wait_ge(s_pv, UNITS * c)
                n0, n1 = band_blocks(c)
                t0 = BLOCKS * c - 1
                sp.dma_start(vw[:, n0:n1, :], v_d[t0 + n0:t0 + n1].rearrange("n p d -> p n d")).then_inc(s_vl, 16)

            def load_cc(c):
                for j in range(CT):
                    sp.wait_ge(s_cst[j], 16 * (c + 1))
                if c > 0:
                    sp.wait_ge(s_l["lo"], CT * c)
                sp.dma_start(cc[:], c_d.rearrange("j p n -> p j n")[:, :, TB * c:TB * (c + 1)]).then_inc(s_cc, 16)

            def load_wo(o):
                if o >= 2:
                    sp.wait_ge(s_wolo, o - 1)
                sp.dma_start(wo_raw[o % 2][:], w_out[o].rearrange("p k n -> p (k n)")).then_inc(s_wor[o % 2], 16)

            def load_weight(n, slot, src):
                sp.wait_ge(s_flo, n + 1)
                sp.dma_start(wraw[slot][:], src).then_inc(s_rw[slot], 16)

            load_xt(0)
            load_x(0)
            sp.dma_start(par[:], params).then_inc(s_par, 16)
            sp.dma_start(ident[:], consts[:, P:2 * P]).then_inc(s_par, 16)
            for f in range(PROJ):
                if f >= 4:
                    sp.wait_ge(s_wlo, f - 3)
                sp.dma_start(w_raw[f % 4], w_in[f].rearrange("p k n -> p (k n)")).then_inc(s_wr[f % 4], 16)
                if f == 3:
                    sp.dma_start(ones[:], consts[:, 0:P]).then_inc(s_ones, 16)
                    sp.dma_start(pick[:], consts[:, C_PICK:C_SPREAD]).then_inc(s_ones, 16)
                    sp.dma_start(spread[:], consts[:, C_SPREAD:C_BIAS]).then_inc(s_ones, 16)
            load_xt(1)
            load_x(1)
            sp.wait_ge(s_set, 1)
            z = zeros[:, 0:CT * HALO].rearrange("p (j n) -> p j n", j=CT)
            u_v = u_d.rearrange("j p n -> p j n")
            for edge in (0, PROMPT_U - HALO, PROMPT_U, U_COLS - HALO):
                sp.dma_start(u_v[:, :, edge:edge + HALO], z).then_inc(s_zst, 16)
            for d in (x2_d, h2_d):
                dv = d.rearrange("k p n -> p k n")
                for a, n in PAD_SPANS:
                    sp.dma_start(dv[:, :, a:a + n], zeros[:, 0:KT * n].rearrange("p (k n) -> p k n", k=KT),
                                 allow_slow_non_contiguous=True).then_inc(s_zst, 16)
            for t in range(STEPS):
                if 1 <= t and t + 1 < STEPS:
                    load_x(t + 1)
                if t == STEPS - 1:
                    sp.wait_ge(s_pj, PROJ * (STEPS - 1))
                    sp.wait_ge(s_hf, KT * STEPS)
                    sp.wait_ge(s_hlo, STEPS)
                    load_cc(0)
                    load_qk(0)
                    sp.dma_start(bias[:], consts[:, C_BIAS:].rearrange("p (h s) -> p h s", h=HEADS)) \
                      .then_inc(s_bias, 16)
                    load_wo(0)
                    load_wo(1)
                sp.wait_ge(s_v, t + 1)
                sp.dma_start(v_d[2 * t:2 * t + 2].rearrange("n p d -> p n d"),
                             vb[:].rearrange("p (n d) -> p n d", n=2)).then_inc(s_vst, 16)
                for m in range(NORMED):
                    if m in GLU_AFTER:
                        store_u(t, GLU_AFTER.index(m))
                    store_qk(t, m)
                store_u(t, 1)
                if t + 2 < STEPS:
                    load_xt(t + 2)
                for j in range(2, CT):
                    store_u(t, j)
            for m in range(NORMED):
                sp.wait_ge(s_qst[m], 16 * STEPS)
            sp.wait_ge(s_vst, 16 * STEPS)
            load_v(0)

            sp.wait_ge(s_pj, PROJ * STEPS)
            sp.dma_start(xb[:], x[:, :, 0:TB]).then_inc(s_xb, 16)
            for o in range(2, KT):
                load_wo(o)
            for c in range(CHUNKS):
                if c + 1 < CHUNKS:
                    load_cc(c + 1)
                    load_qk(c + 1)
                    load_v(c + 1)
                else:
                    sp.wait_ge(s_pv, UNITS * CHUNKS)
                    sp.wait_ge(s_l["lo"], CT * CHUNKS)
                    for i in range(4):
                        sp.wait_ge(s_cst[i], 16 * CHUNKS)
                    sp.wait_ge(s_h2st[0], 16 * KT // 2)
                    sp.wait_ge(s_h2st[1], 16 * KT // 2)
                    sp.wait_ge(s_zst, 16 * ZERO_STORES)
                    sp.dma_start(hw_raw[:], h2_d.rearrange("k p n -> p k n")[:, :, 0:TH]).then_inc(s_hw, 16)
                    for n in range(2):
                        sp.dma_start(wraw[n][:], w_ffn[n]).then_inc(s_rw[n], 16)
                sp.wait_ge(s_x2, KT * (c + 1))
                sp.dma_start(x2_d.rearrange("k p n -> p k n")[:, :, padded(c):padded(c) + TB], xb[:]) \
                  .then_inc(s_x2st, 16)
                if c + 1 == CHUNKS:
                    sp.wait_ge(s_wo, KT * CHUNKS)
                    for n in range(2, 2 * RING):
                        load_weight(n, n % RING, w_ffn[n])
                for k in range(KT):
                    sp.wait_ge(s_h2, KT * c + k + 1)
                    sp.dma_start(h2_d[k, :, padded(c):padded(c) + TB], tmp[k % 2][:]).then_inc(s_h2st[k % 2], 16)
                if c + 1 < CHUNKS:
                    sp.wait_ge(s_x2st, 16 * (c + 1))
                    sp.dma_start(xb[:], x[:, :, TB * (c + 1):TB * (c + 2)]).then_inc(s_xb, 16)

            sp.wait_ge(s_x2st, 16 * CHUNKS)
            for i in range(2):
                sp.wait_ge(s_h2st[i], 16 * KT // 2 * CHUNKS)
            for w in range(WINDOWS):
                base = TILES_W * w
                with sp.Fori(2 if w == 0 else 0, FT // 2) as i:
                    for s in range(4):
                        load_weight(base + 4 * i + s, s, w_ffn[bass.ds(4 * i + s, 1)].rearrange("o p k n -> (o p) k n"))
                for o in range(KT):
                    for s in range(DOWN_PIECES):
                        n = DOWN_PIECES * o + s
                        load_weight(base + TILES_F + n, n % RING, w_down[o, s])
                    if KT * w + o >= 2:
                        sp.wait_ge(s_y, KT * w + o - 1)
                    sp.dma_start(x2w[o % 2][:], x2_d[o, :, 1 + TC * w:1 + TC * (w + 1)]).then_inc(s_x2w[o % 2], 16)
                    if o == 1 and w + 1 < WINDOWS:
                        sp.wait_ge(s_hwlo, w + 1)
                        sp.dma_start(hw_raw[:], h2_d.rearrange("k p n -> p k n")[:, :, TC * (w + 1):TC * (w + 1) + TH]) \
                          .then_inc(s_hw, 16)

        @block.gpsimd
        def _(pool):
            def load_window(unit):
                c, j = divmod(unit, CT)
                if j == 0:
                    last = 2 * c + (1 if c in (0, CHUNKS - 1) else 2)
                    pool.wait_ge(s_ust[0], 16 * (CT // 2) * (last + 1))
                    pool.wait_ge(s_ust[1], 16 * (CT // 2) * (last + 1))
                if unit == 0:
                    pool.wait_ge(s_zst, 16 * ZERO_STORES)
                if unit >= 4:
                    pool.wait_ge(s_cv, unit_last_op(unit - 4) + 1)
                pool.dma_start(conv_win[unit % 4][:], u_d[j, :, u_window(c):u_window(c) + TB + 2 * HALO]) \
                    .then_inc(s_win[unit % 4], 16)

            for unit in range(4):
                load_window(unit)
            for unit in range(CONV_UNITS):
                c, j = divmod(unit, CT)
                pool.wait_ge(s_cv, unit_last_op(unit) + 1)
                pool.dma_start(c_d[j, :, TB * c:TB * (c + 1)], conv_acc[unit % 4][:]).then_inc(s_cst[unit % 4], 16)
                if unit + 4 < CONV_UNITS:
                    load_window(unit + 4)

            for w in range(WINDOWS):
                for o in range(KT):
                    pool.wait_ge(s_y, KT * w + o + 1)
                    pool.dma_start(y[o, :, TC * w:TC * (w + 1)], yb[o % 2][:]).then_inc(s_yst[o % 2], 16)
            for i in range(2):
                pool.wait_ge(s_yst[i], 16 * WINDOWS * KT // 2)

        @block.scalar
        def _(act):
            def token_squares(t):
                act.wait_ge(s_xt, 16 * (t + 1))
                for b in range(TA // P):
                    nc.scalar.activation(xt[:, b, :], xt[:, b, :], ACT.Square,
                                         accum_out=t_ss[t % 2][:, b:b + 1]).then_inc(s_tsq, 1)

            def token_root(t):
                act.wait_ge(s_tsq, TA // P * (t + 1))
                if t >= 2:
                    act.wait_ge(s_trs, t - 1)
                nc.scalar.activation(t_rt[t % 2][:], t_ss[t % 2][:], ACT.Sqrt, bias=eps[:, 0:1],
                                     scale=1.0 / D_MODEL).then_inc(s_trt, 1)

            def h_high(t):
                act.wait_ge(s_hf, KT * (t + 1))
                if t >= 2:
                    act.wait_ge(s_pj, PROJ * (t - 1))
                if t == 1:
                    act.wait_ge(s_wlo, PROJ)
                nc.scalar.activation(h_hi[t % 2][:], hb[:], ACT.Copy).then_inc(s_hhi, 1)

            def qk_square(t, m):
                M = NORMED * t + m
                act.wait_ge(s_pj, PROJ * t + m + 1)
                if M >= 2:
                    act.wait_ge(s_qss, M - 1)
                if t > 0:
                    act.wait_ge(s_qst[m], 16 * t)
                nc.scalar.activation(qk[m][:], proj_bank(PROJ * t + m), ACT.Copy).then_inc(s_qc, 1)
                nc.scalar.activation(q_sq[M % 2][:], proj_bank(PROJ * t + m), ACT.Square).then_inc(s_qs, 1)

            def qk_root(t):
                act.wait_ge(s_qss, NORMED * (t + 1))
                if t > 0:
                    act.wait_ge(s_qri, t)
                nc.scalar.activation(q_root[0:NORM_ROWS, :], bank[5][0:NORM_ROWS, 0:TA], ACT.Sqrt,
                                     bias=eps[0:NORM_ROWS, 0:1], scale=1.0 / HEAD_DIM).then_inc(s_qrt, 1)

            def ln_mean(c):
                act.wait_ge(s_l["sum"], c + 1)
                if c > 0:
                    act.wait_ge(s_l["scaled"], c)
                nc.scalar.activation(ln_st[:], bank[6][:], ACT.Copy, scale=1.0 / CONV_W).then_inc(s_l["mean"], 1)

            def ln_squares(c, half):
                act.wait_ge(s_l["centred"], c + 1)
                if c == 0 and not half:
                    for m in range(NORMED):
                        act.wait_ge(s_qst[m], 16 * STEPS)
                for j in (2 * half, 2 * half + 1):
                    if half:
                        act.wait_ge(s_l["sq_added"], (CT - 1) * c + 1)
                    elif c > 1:
                        act.wait_ge(s_h2st[j], 16 * KT // 2 * (c - 1))
                    elif c == 0 and j == 1:
                        act.wait_ge(s_qsp, NORMED * STEPS)
                    nc.scalar.activation(tmp[j % 2][:], cc[:, j, :], ACT.Square).then_inc(s_l["squared"], 1)

            def ln_scale(c):
                act.wait_ge(s_l["var"], c + 1)
                nc.scalar.activation(ln_st[:], bank[6][:], ACT.Ln, bias=eps[:, 1:2],
                                     scale=1.0 / CONV_W).then_inc(s_l["log"], 1)
                act.wait_ge(s_l["log"], c + 1)
                nc.scalar.activation(ln_st[:], ln_st[:], ACT.Exp, scale=-0.5).then_inc(s_l["scale"], 1)

            def ln_swish(c):
                act.wait_ge(s_l["scaled"], c + 1)
                for j in range(CT):
                    nc.scalar.activation(cc[:, j, :], cc[:, j, :], ACT.Silu, bias=col("ln_b", j),
                                         scale=col("ln_g", j)).then_inc(s_l["swish"], 1)

            def ln_high(c, j):
                act.wait_ge(s_l["swish"], CT * c + j + 1)
                if c > 0:
                    act.wait_ge(s_wo, KT * c)
                nc.scalar.activation(cat_hi[:, AT + j, :], cc[:, j, :], ACT.Copy).then_inc(s_l["hi"], 1)

            def wo_high(o):
                act.wait_ge(s_wor[o % 2], 16 * (o // 2 + 1))
                nc.scalar.activation(wo_hi[:, o].rearrange("p k n -> p (k n)"), wo_raw[o % 2][:], ACT.Copy) \
                  .then_inc(s_wohi, 1)

            act.wait_ge(s_set, 4)
            token_squares(0)
            act.wait_ge(s_wr[0], 16)
            nc.scalar.activation(win_hi[:, 0].rearrange("p k n -> p (k n)"), w_raw[0], ACT.Copy).then_inc(s_whi, 1)
            token_root(0)
            for f in range(1, PROJ):
                if f == 3:
                    h_high(0)
                act.wait_ge(s_wr[f % 4], 16 * (f // 4 + 1))
                nc.scalar.activation(win_hi[:, f].rearrange("p k n -> p (k n)"), w_raw[f % 4], ACT.Copy) \
                  .then_inc(s_whi, 1)
                if f in SQUARE_AFTER:
                    qk_square(0, SQUARE_AFTER.index(f))
            token_squares(1)
            for t in range(STEPS):
                last = t == STEPS - 1
                for m in range(len(SQUARE_AFTER) if t == 0 else 0, NORMED):
                    qk_square(t, m)
                act.wait_ge(s_pj, PROJ * t + F_V + 1)
                if t > 0:
                    act.wait_ge(s_u, CT * t)
                nc.scalar.activation(v_raw[:], proj_bank(PROJ * t + F_V), ACT.Copy).then_inc(s_vr, 1)
                qk_root(t)
                if not last:
                    token_root(t + 1)
                act.wait_ge(s_vt, t + 1)
                act.wait_ge(s_qri, t + 1)
                if t > 0:
                    act.wait_ge(s_vst, 16 * t)
                nc.scalar.activation(vb[:], bank[6][:, TA:2 * TA], ACT.Copy).then_inc(s_v, 1)
                for j in range(CT):
                    n = PROJ * t + F_G + 2 * j + 1
                    act.wait_ge(s_pj, n + 1)
                    if CT * t + j >= 2:
                        act.wait_ge(s_u, CT * t + j - 1)
                    nc.scalar.activation(sig[j % 2][:], proj_bank(n), ACT.Sigmoid).then_inc(s_sig, 1)
                    if last and j == 1:
                        ln_mean(0)
                    if last and j == 2:
                        ln_squares(0, 0)
                    if last and j == 3:
                        ln_squares(0, 1)
                    if not last and j == 0:
                        h_high(t + 1)
                if t + 2 < STEPS:
                    token_squares(t + 2)

            def exps(U):
                act.wait_ge(s_nm, U + 1)
                if U >= 2:
                    act.wait_ge(s_dn, U - 1)
                ks = unit_of(U)[3]
                for t in range(GROUP):
                    s_ = S[U % 2][:, t, P * ks[0]:P * (ks[-1] + 1)]
                    nc.scalar.activation(s_, s_, ACT.Exp, bias=nm4[U % 2][:, t:t + 1],
                                         accum_out=rs4[U % 2][:, t:t + 1]).then_inc(s_ex, 1)
                act.wait_ge(s_es, U + 1)
                nc.scalar.activation(ee4[U % 2][:], es4[U % 2][:], ACT.Exp).then_inc(s_ee, 1)

            def normalise(U):
                act.wait_ge(s_ri, U + 1)
                ks = unit_of(U)[3]
                for t in range(GROUP):
                    p_ = S[U % 2][:, t, P * ks[0]:P * (ks[-1] + 1)]
                    nc.scalar.activation(p_, p_, ACT.Copy, scale=ri4[U % 2][:, t:t + 1]).then_inc(s_p, 1)

            def copy_t(U, kt):
                if U >= 2:
                    act.wait_ge(s_pv, U - 1)
                act.wait_ge(s_t, t_seq[U, kt] + 1)
                nc.scalar.activation(PT[U % 2][:, kt, :], bank[4 + t_seq[U, kt] % 2][:], ACT.Copy).then_inc(s_pt, 1)

            def attn_high(U):
                c, n, g, _ = unit_of(U)
                act.wait_ge(s_pv, U + 1)
                if c > 0 and n == 0:
                    act.wait_ge(s_wo, KT * c)
                rows = slice(HEAD_DIM * g, HEAD_DIM * (g + 1))
                nc.scalar.activation(cat_hi[rows, 0:AT, P * n:P * (n + 1)],
                                     bank[7][rows, :].rearrange("p (t q) -> p t q", t=AT), ACT.Copy) \
                  .then_inc(s_ahi, 1)

            def norm2_log(c):
                act.wait_ge(s_n2m, c + 1)
                nc.scalar.activation(n2_rs[:], bank[6][:], ACT.Ln, bias=eps[:, 0:1],
                                     scale=1.0 / D_MODEL).then_inc(s_n2l, 1)

            def norm2_scale(c):
                act.wait_ge(s_n2l, c + 1)
                nc.scalar.activation(n2_rs[:], n2_rs[:], ACT.Exp, scale=-0.5).then_inc(s_n2s, 1)

            def weight_high(n, slot, turn):
                act.wait_ge(s_rw[slot], 16 * (turn + 1))
                act.wait_ge(s_used, n + 1)
                nc.scalar.activation(whi[slot][:], wraw[slot][:], ACT.Copy).then_inc(s_fhi, 1)

            def window_high(w):
                act.wait_ge(s_hw, 16 * (w + 1))
                if w > 0:
                    act.wait_ge(s_used, RING + TILES_W * (w - 1) + TILES_F)
                nc.scalar.activation(hw_hi[:], hw_raw[:], ACT.Copy).then_inc(s_hwhi, 1)

            exps(0)
            normalise(0)
            ln_scale(0)
            exps(1)
            for c in range(CHUNKS):
                for u in range(UNITS):
                    U = UNITS * c + u
                    for kt in kts(c, u // KV_HEADS):
                        copy_t(U, kt)
                        if kt == 1 and u > 0:
                            attn_high(U - 1)
                    if u + 1 < UNITS:
                        normalise(U + 1)
                    if c == 0:
                        wo_high(u)
                    if c == 0 and u == 2:
                        ln_swish(0)
                    if c > 0 and u == 1:
                        norm2_log(c - 1)
                    if c > 0 and u == 2:
                        norm2_scale(c - 1)
                    if 3 <= u < 3 + CT:
                        ln_high(c, u - 3)
                    if u + 2 < UNITS:
                        exps(U + 2)
                attn_high(UNITS * c + UNITS - 1)
                more = c + 1 < CHUNKS
                for o in range(KT):
                    n = KT * c + o
                    act.wait_ge(s_x2, n + 1)
                    if o >= 2:
                        act.wait_ge(s_n2a, (KT - 1) * c + max(o - 2, 1))
                    elif c == 0:
                        act.wait_ge(s_wolo, KT)
                    else:
                        act.wait_ge(s_n2a, (KT - 1) * c)
                    nc.scalar.activation(sq[o % 2][:], xb[:, o, :], ACT.Square).then_inc(s_x2q, 1)
                    if more:
                        if o == 1:
                            ln_mean(c + 1)
                            ln_squares(c + 1, 0)
                        if o == 2:
                            ln_squares(c + 1, 1)
                        if o == 3:
                            exps(UNITS * (c + 1))
                        if o == 4:
                            normalise(UNITS * (c + 1))
                        if o == 5:
                            ln_scale(c + 1)
                            exps(UNITS * (c + 1) + 1)
                            ln_swish(c + 1)
                    else:
                        if o == 1:
                            act.sem_inc(s_gb, 2)
                            window_high(0)
                        if o in (2, 3):
                            weight_high(o - 2, o - 2, 0)

            def gate_up(w, i, s):
                base, turns = TILES_W * w, TILES_W // RING * w
                J = FT * w + 2 * i + s
                for r in range(2):
                    tile = 2 * s + 2 + r
                    weight_high(base + 4 * i + tile, tile % RING, turns + i + tile // RING)
                act.wait_ge(s_used, RING + base + 4 * i + 2 * s + 1)
                act.wait_ge(s_c3, J + 1)
                nc.scalar.activation(gb[s][:], bank[s][:, 0:TH], ACT.Copy).then_inc(s_gb, 1)
                act.wait_ge(s_c3, J + 3)
                nc.scalar.activation(cv[s][:], cv[s][:], ACT.Silu).then_inc(s_sl, 1)
                act.wait_ge(s_m, J + 3)
                nc.scalar.activation(mid_hi(2 * i + s), mb[s][:], ACT.Copy).then_inc(s_mhi, 1)

            gate_up(0, 0, 0)
            norm2_log(CHUNKS - 1)
            norm2_scale(CHUNKS - 1)
            gate_up(0, 0, 1)
            for w in range(WINDOWS):
                base = TILES_W * w
                turns = TILES_W // RING * w
                with act.Fori(1 if w == 0 else 0, FT // 2) as i:
                    for s in range(2):
                        gate_up(w, i, s)
                for o in range(KT):
                    for s in range(DOWN_PIECES):
                        n = TILES_F + DOWN_PIECES * o + s + 2
                        if base + n < TILES_W * WINDOWS:
                            weight_high(base + n, n % RING, turns + n // RING)
                    if o == 2 and w + 1 < WINDOWS:
                        window_high(w + 1)

        @block.vector
        def _(dve):
            def conv_ops(first, count):
                for m in range(first, min(first + count, CONV_OPS)):
                    two, r = divmod(m, PAIR_OPS)
                    tap, unit = r // 2, 2 * two + r % 2
                    j = unit % CT
                    win, acc = conv_win[unit % 4], conv_acc[unit % 4]
                    w_tap = par[:, PARAM_AT["conv_w"] + TAPS * j + tap:PARAM_AT["conv_w"] + TAPS * j + tap + 1]
                    if tap == 0:
                        dve.wait_ge(s_win[unit % 4], 16 * (unit // 4 + 1))
                        if unit >= 4:
                            dve.wait_ge(s_cst[unit % 4], 16 * (unit // 4))
                        nc.vector.tensor_scalar(acc[:], win[:, 0:TB], w_tap, col("conv_b", j), ALU.mult, ALU.add) \
                          .then_inc(s_cv, 1)
                    else:
                        dve.wait_ge(s_cv, m - 1)
                        nc.vector.scalar_tensor_tensor(acc[:], win[:, tap:tap + TB], w_tap, acc[:],
                                                       ALU.mult, ALU.add).then_inc(s_cv, 1)

            def conv_slot(t, i, slots):
                lo, hi = CONV_A[t] * i // slots, CONV_A[t] * (i + 1) // slots
                conv_ops(sum(CONV_A[:t]) + lo, hi - lo)

            nc.vector.memset(zeros, 0.0).then_inc(s_set, 1)
            nc.vector.memset(eps[:, 0:1], 1e-6).then_inc(s_set, 1)
            nc.vector.memset(eps[:, 1:2], 1e-5).then_inc(s_set, 1)
            dve.wait_ge(s_par, 32)
            nc.vector.tensor_scalar(qg[:], col("q_g"), HEAD_DIM ** -0.5, None, ALU.mult).then_inc(s_set, 1)

            def w_low(f):
                dve.wait_ge(s_whi, f + 1)
                nc.vector.tensor_tensor(win_lo[:, f].rearrange("p k n -> p (k n)"), w_raw[f % 4],
                                        win_hi[:, f].rearrange("p k n -> p (k n)").bitcast(F32), ALU.subtract) \
                  .then_inc(s_wlo, 1)

            def norm_h(t):
                dve.wait_ge(s_nst, t + 1)
                dve.wait_ge(s_x[t % 2], 16 * (t // 2 + 1))
                if t > 0:
                    dve.wait_ge(s_hlo, t)
                for k in range(KT):
                    nc.vector.scalar_tensor_tensor(hb[:, k, :], xs[t % 2][:, k, :], col("g1", k), bank[6][:, 0:TA],
                                                   ALU.mult, ALU.mult).then_inc(s_hf, 1)

            def h_low(t):
                dve.wait_ge(s_hhi, t + 1)
                nc.vector.tensor_tensor(h_lo[t % 2][:], hb[:], h_hi[t % 2][:].bitcast(F32), ALU.subtract) \
                  .then_inc(s_hlo, 1)

            def token_inverse(t):
                dve.wait_ge(s_trt, t + 1)
                if t >= 2:
                    dve.wait_ge(s_nst, t - 1)
                nc.vector.reciprocal(t_rs[t % 2][:], t_rt[t % 2][:]).then_inc(s_trs, 1)

            def qk_inverse(t):
                dve.wait_ge(s_qrt, t + 1)
                if t > 0:
                    dve.wait_ge(s_qsp, NORMED * t)
                nc.vector.reciprocal(q_inv[0:NORM_ROWS, :], q_root[0:NORM_ROWS, :]).then_inc(s_qri, 1)

            def qk_norm(t, m):
                M = NORMED * t + m
                dve.wait_ge(s_qc, M + 1)
                dve.wait_ge(s_qsp, M + 1)
                nc.vector.scalar_tensor_tensor(qk[m][:], qk[m][:], col("k_g") if m == 0 else qg[:, 0:1],
                                               spread_bank[m % 2][:, 0:TA], ALU.mult, ALU.mult).then_inc(s_qn, 1)

            def glu(t, j):
                g = CT * t + j
                dve.wait_ge(s_sig, g + 1)
                if g >= 2:
                    dve.wait_ge(s_ust[j % 2], 16 * (g // 2))
                nc.vector.tensor_tensor(ub[j % 2][:], proj_bank(PROJ * t + F_G + 2 * j), sig[j % 2][:], ALU.mult) \
                  .then_inc(s_u, 1)

            def ln_add(c):
                dve.wait_ge(s_cc, 16 * (c + 1))
                if c > 0:
                    dve.wait_ge(s_l["var"], c)
                nc.vector.tensor_tensor(ln_acc[:], cc[:, 0, :], cc[:, 1, :], ALU.add).then_inc(s_l["added"], 1)
                for j in range(2, CT):
                    dve.wait_ge(s_l["added"], (CT - 1) * c + j - 1)
                    nc.vector.tensor_tensor(ln_acc[:], ln_acc[:], cc[:, j, :], ALU.add).then_inc(s_l["added"], 1)

            def ln_centre(c):
                dve.wait_ge(s_l["mean"], c + 1)
                nc.vector.tensor_tensor(cc[:], cc[:], ln_st[:].rearrange("p (o n) -> p o n", o=1)
                                        .to_broadcast([P, CT, TB]), ALU.subtract).then_inc(s_l["centred"], 1)

            def ln_add_squares(c, half):
                n = (CT - 1) * c
                if not half:
                    dve.wait_ge(s_l["squared"], CT * c + 2)
                    nc.vector.tensor_tensor(ln_acc[:], tmp[0][:], tmp[1][:], ALU.add).then_inc(s_l["sq_added"], 1)
                else:
                    for j in (2, 3):
                        dve.wait_ge(s_l["squared"], CT * c + j + 1)
                        dve.wait_ge(s_l["sq_added"], n + j - 1)
                        nc.vector.tensor_tensor(ln_acc[:], ln_acc[:], tmp[j % 2][:], ALU.add) \
                          .then_inc(s_l["sq_added"], 1)

            def ln_apply(c):
                dve.wait_ge(s_l["scale"], c + 1)
                nc.vector.tensor_tensor(cc[:], cc[:], ln_st[:].rearrange("p (o n) -> p o n", o=1)
                                        .to_broadcast([P, CT, TB]), ALU.mult).then_inc(s_l["scaled"], 1)

            def ln_low(c, j):
                dve.wait_ge(s_l["hi"], CT * c + j + 1)
                nc.vector.tensor_tensor(cat_lo[:, AT + j, :], cc[:, j, :], cat_hi[:, AT + j, :].bitcast(F32),
                                        ALU.subtract).then_inc(s_l["lo"], 1)

            w_low(0)
            token_inverse(0)
            w_low(1)
            norm_h(0)
            w_low(2)
            h_low(0)
            for f in range(3, PROJ):
                w_low(f)
            slots = 14
            for t in range(STEPS):
                last = t == STEPS - 1
                for i in range(8):
                    conv_slot(t, i, slots)
                qk_inverse(t)
                if not last:
                    token_inverse(t + 1)
                conv_slot(t, 8, slots)
                glu(t, 0)
                qk_norm(t, 0)
                qk_norm(t, 1)
                if not last:
                    norm_h(t + 1)
                else:
                    ln_add(0)
                conv_slot(t, 9, slots)
                for m in range(2, NORMED):
                    qk_norm(t, m)
                glu(t, 1)
                conv_slot(t, 10, slots)
                if not last:
                    h_low(t + 1)
                else:
                    ln_centre(0)
                conv_slot(t, 11, slots)
                glu(t, 2)
                if last:
                    ln_add_squares(0, 0)
                conv_slot(t, 12, slots)
                glu(t, 3)
                if last:
                    ln_add_squares(0, 1)
                conv_slot(t, 13, slots)

            def add_bias(U):
                c, n, g, ks = unit_of(U)
                cols = slice(P * ks[0], P * (ks[-1] + 1))
                if U >= 2:
                    dve.wait_ge(s_t, t_end(U - 2))
                if U == 0:
                    dve.wait_ge(s_bias, 16)
                    dve.wait_ge(s_pj, PROJ * STEPS)
                for t in range(GROUP):
                    dve.wait_ge(s_qk, GROUP * U + t + 1)
                    nc.vector.tensor_tensor_reduce(out=S[U % 2][:, t, cols], in0=bank[t][:, cols],
                                                   in1=bias[:, GROUP * g + t, cols], scale=1.0, scalar=NEG,
                                                   op0=ALU.add, op1=ALU.max, accum_out=mx[U % 2][:, t:t + 1]) \
                      .then_inc(s_sb, 1)
                sink = par[:, PARAM_AT["sink"] + GROUP * g:PARAM_AT["sink"] + GROUP * (g + 1)]
                dve.wait_ge(s_sb, GROUP * (U + 1))
                nc.vector.tensor_tensor(m4[U % 2][:], mx[U % 2][:], sink, ALU.max).then_inc(s_m4, 1)
                dve.wait_ge(s_m4, U + 1)
                nc.vector.tensor_scalar(nm4[U % 2][:], m4[U % 2][:], -1.0, None, ALU.mult).then_inc(s_nm, 1)
                nc.vector.tensor_tensor(es4[U % 2][:], sink, m4[U % 2][:], ALU.subtract).then_inc(s_es, 1)

            def invert_sums(U):
                dve.wait_ge(s_ex, GROUP * (U + 1))
                dve.wait_ge(s_ee, U + 1)
                nc.vector.tensor_tensor(dn4[U % 2][:], rs4[U % 2][:], ee4[U % 2][:], ALU.add).then_inc(s_dn, 1)
                dve.wait_ge(s_dn, U + 1)
                nc.vector.reciprocal(ri4[U % 2][:], dn4[U % 2][:]).then_inc(s_ri, 1)

            def attn_low(U):
                c, n, g, _ = unit_of(U)
                rows = slice(HEAD_DIM * g, HEAD_DIM * (g + 1))
                dve.wait_ge(s_ahi, U + 1)
                nc.vector.tensor_tensor(cat_lo[rows, 0:AT, P * n:P * (n + 1)],
                                        bank[7][rows, :].rearrange("p (t q) -> p t q", t=AT),
                                        cat_hi[rows, 0:AT, P * n:P * (n + 1)].bitcast(F32), ALU.subtract) \
                  .then_inc(s_alo, 1)

            def wo_low(o):
                dve.wait_ge(s_wohi, o + 1)
                nc.vector.tensor_tensor(wo_lo[:, o].rearrange("p k n -> p (k n)"), wo_raw[o % 2][:],
                                        wo_hi[:, o].rearrange("p k n -> p (k n)").bitcast(F32), ALU.subtract) \
                  .then_inc(s_wolo, 1)

            def norm2_add(c, o):
                n = (KT - 1) * c + o
                dve.wait_ge(s_x2q, KT * c + o + 1)
                if o == 1:
                    if c > 0:
                        dve.wait_ge(s_n2m, c)
                    nc.vector.tensor_tensor(n2_acc[:], sq[0][:], sq[1][:], ALU.add).then_inc(s_n2a, 1)
                else:
                    dve.wait_ge(s_n2a, n - 1)
                    nc.vector.tensor_tensor(n2_acc[:], n2_acc[:], sq[o % 2][:], ALU.add).then_inc(s_n2a, 1)

            def norm2_apply(c, ks):
                dve.wait_ge(s_n2s, c + 1)
                for k in ks:
                    n = KT * c + k
                    if n >= 2:
                        dve.wait_ge(s_h2st[k % 2], 16 * (n // 2))
                    nc.vector.scalar_tensor_tensor(tmp[k % 2][:], xb[:, k, :], col("g2", k), n2_rs[:],
                                                   ALU.mult, ALU.mult).then_inc(s_h2, 1)

            def weight_low(n, slot):
                dve.wait_ge(s_fhi, n + 1)
                nc.vector.tensor_tensor(wlo[slot][:], wraw[slot][:], whi[slot][:].bitcast(F32), ALU.subtract) \
                  .then_inc(s_flo, 1)

            def window_low(w):
                dve.wait_ge(s_hwhi, w + 1)
                nc.vector.tensor_tensor(hw_lo[:], hw_raw[:], hw_hi[:].bitcast(F32), ALU.subtract).then_inc(s_hwlo, 1)

            add_bias(0)
            add_bias(1)
            for i in range(2):
                dve.wait_ge(s_ust[i], 16 * CT * STEPS // 2)
            dve.wait_ge(s_vst, 16 * STEPS)
            invert_sums(0)
            ln_apply(0)
            conv_at = sum(CONV_A)
            for c in range(CHUNKS):
                more = c + 1 < CHUNKS
                for u in range(UNITS):
                    U = UNITS * c + u
                    if u + 1 < UNITS:
                        invert_sums(U + 1)
                    if u > 0:
                        attn_low(U - 1)
                    if u + 2 < UNITS:
                        add_bias(U + 2)
                    if 4 <= u < 4 + CT:
                        ln_low(c, u - 4)
                    conv_ops(conv_at, CONV_B_UNITS[c][u])
                    conv_at += CONV_B_UNITS[c][u]
                    if c == 0:
                        wo_low(u)
                    elif 2 <= u < 6:
                        norm2_apply(c - 1, (2 * u - 4, 2 * u - 3))
                attn_low(UNITS * c + UNITS - 1)
                for o in range(KT):
                    n = KT * c + o
                    dve.wait_ge(s_wo, n + 1)
                    if o == 0:
                        dve.wait_ge(s_xb, 16 * (c + 1))
                    nc.vector.tensor_tensor(xb[:, o, :], bank[OUT_BANKS[o]][:], xb[:, o, :], ALU.add) \
                      .then_inc(s_x2, 1)
                    if o >= 2:
                        norm2_add(c, o - 1)
                    if more:
                        if o == 0:
                            ln_add(c + 1)
                        if o == 2:
                            ln_add_squares(c + 1, 0)
                        if o == 3:
                            ln_add_squares(c + 1, 1)
                            add_bias(UNITS * (c + 1))
                        if o == 4:
                            invert_sums(UNITS * (c + 1))
                        if o == 5:
                            add_bias(UNITS * (c + 1) + 1)
                            ln_apply(c + 1)
                    else:
                        if o == 1:
                            dve.sem_inc(s_flo, RING)
                            window_low(0)
                        if o in (2, 3):
                            weight_low(o - 2, o - 2)
                    if c < CONV_B_CHUNKS:
                        conv_ops(conv_at, CONV_B_OUT[o])
                        conv_at += CONV_B_OUT[o]
                    if more and o == 1:
                        ln_centre(c + 1)
                norm2_add(c, KT - 1)

            def gate_up(w, i, s):
                base = TILES_W * w
                J = FT * w + 2 * i + s
                taps = [ffn_w_ap[:, bass.ds((2 * i + s) * FFN_TAPS + r, 1)] for r in range(FFN_TAPS)]
                b_ = par[:, bass.ds(2 * i + s + PARAM_AT["ffn_b"], 1)]
                for r in range(2):
                    tile = 2 * s + 2 + r
                    weight_low(base + 4 * i + tile, tile % RING)
                dve.wait_ge(s_gb, J + 3)
                dve.wait_ge(s_m, J + 1)
                nc.vector.tensor_scalar(cv[s][:], gb[s][:, 0:TC], taps[0], b_, ALU.mult, ALU.add).then_inc(s_c1, 1)
                dve.wait_ge(s_c1, J + 1)
                nc.vector.scalar_tensor_tensor(cv[s][:], gb[s][:, 1:TC + 1], taps[1], cv[s][:],
                                               ALU.mult, ALU.add).then_inc(s_c2, 1)
                dve.wait_ge(s_c2, J + 1)
                nc.vector.scalar_tensor_tensor(cv[s][:], gb[s][:, 2:TC + 2], taps[2], cv[s][:],
                                               ALU.mult, ALU.add).then_inc(s_c3, 1)
                dve.wait_ge(s_sl, J + 1)
                dve.wait_ge(s_used, RING + base + 4 * i + 2 * s + 2)
                dve.wait_ge(s_mlo, J + 1)
                nc.vector.tensor_tensor(mb[s][:], bank[2 + s][:, 0:TC], cv[s][:], ALU.mult).then_inc(s_m, 1)
                dve.wait_ge(s_mhi, J + 1)
                nc.vector.tensor_tensor(mid_lo(2 * i + s), mb[s][:], mid_hi(2 * i + s).bitcast(F32), ALU.subtract) \
                  .then_inc(s_mlo, 1)

            dve.sem_inc(s_c3, 2)
            dve.sem_inc(s_m, 2)
            dve.sem_inc(s_mlo, 2)
            gate_up(0, 0, 0)
            norm2_apply(CHUNKS - 1, range(KT // 2))
            gate_up(0, 0, 1)
            norm2_apply(CHUNKS - 1, range(KT // 2, KT))
            dve.wait_ge(s_x2st, 16 * CHUNKS)
            for i in range(2):
                dve.wait_ge(s_h2st[i], 16 * KT // 2 * CHUNKS)
            for w in range(WINDOWS):
                base = TILES_W * w
                with dve.Fori(1 if w == 0 else 0, FT // 2) as i:
                    for s in range(2):
                        gate_up(w, i, s)
                for o in range(KT):
                    n = KT * w + o
                    for s in range(DOWN_PIECES):
                        tile = TILES_F + DOWN_PIECES * o + s + 2
                        if base + tile < TILES_W * WINDOWS:
                            weight_low(base + tile, tile % RING)
                    if o == 2 and w + 1 < WINDOWS:
                        window_low(w + 1)
                    dve.wait_ge(s_used, RING + base + TILES_F + DOWN_PIECES * (o + 1))
                    dve.wait_ge(s_x2w[o % 2], 16 * (n // 2 + 1))
                    if n >= 2:
                        dve.wait_ge(s_yst[o % 2], 16 * (n // 2))
                    nc.vector.tensor_tensor(yb[o % 2][:], bank[4 + o % 2][:, 0:TC], x2w[o % 2][:], ALU.add) \
                      .then_inc(s_y, 1)

        @block.tensor
        def _(pe):
            def spread_scale(t):
                pe.wait_ge(s_trs, t + 1)
                pe.wait_ge(s_v, t)
                if t > 0:
                    pe.wait_ge(s_hf, KT * t)
                for b in range(TA // P):
                    mm = nc.tensor.matmul(bank[6][:, P * b:P * (b + 1)], t_rs[t % 2][:, b:b + 1].to_broadcast([P, P]),
                                          ident[:], start=True, stop=True)
                mm.then_inc(s_nst, 1)

            def bank_free(n):
                t, f = divmod(n, PROJ)
                if f < NORMED:
                    pe.wait_ge(s_qs, NORMED * t + f + 1)
                elif f == F_V:
                    pe.wait_ge(s_vr, t + 1)
                elif (f - F_G) % 2 == 0:
                    pe.wait_ge(s_u, CT * t + (f - F_G) // 2 + 1)
                else:
                    pe.wait_ge(s_sig, CT * t + (f - F_G) // 2 + 1)

            def project(t, f):
                n = PROJ * t + f
                if n >= SLOTS:
                    bank_free(n - SLOTS)
                if t == 0:
                    pe.wait_ge(s_wlo, f + 1)
                if f == 0:
                    pe.wait_ge(s_hlo, t + 1)
                hi, lo = h_hi[t % 2], h_lo[t % 2]
                i = 0
                for k in range(KT):
                    for l, r in ((win_hi, hi), (win_hi, lo), (win_lo, hi)):
                        mm = nc.tensor.matmul(proj_bank(n), l[:, f, k, :], r[:, k, :], start=(i == 0), stop=(i == 3 * KT - 1))
                        i += 1
                mm.then_inc(s_pj, 1)

            def transpose_v(t):
                pe.wait_ge(s_vr, t + 1)
                pe.wait_ge(s_hf, KT * (t + 1))
                for b in range(TA // P):
                    mm = nc.tensor.transpose(bank[6][:, TA + P * b:TA + P * (b + 1)], v_raw[:, P * b:P * (b + 1)], ident[:])
                mm.then_inc(s_vt, 1)

            def qk_sum(t, m):
                pe.wait_ge(s_qs, NORMED * t + m + 1)
                if m == 0 and t > 0:
                    pe.wait_ge(s_qn, NORMED * t)
                at0 = NORM_ROWS - KV_HEADS * (m + 1)
                nc.tensor.matmul(bank[5][0:NORM_ROWS, 0:TA], pick[:, at0:at0 + NORM_ROWS], q_sq[(NORMED * t + m) % 2][:],
                                 start=(m == 0), stop=(m == NORMED - 1)).then_inc(s_qss, 1)

            def qk_spread(t, m):
                M = NORMED * t + m
                pe.wait_ge(s_qri, t + 1)
                if M >= 2:
                    pe.wait_ge(s_qn, M - 1)
                nc.tensor.matmul(spread_bank[m % 2][:, 0:TA],
                                 spread[0:NORM_ROWS, P * m:P * (m + 1)], q_inv[0:NORM_ROWS, :],
                                 start=True, stop=True).then_inc(s_qsp, 1)

            def ln_sum(c):
                pe.wait_ge(s_l["added"], (CT - 1) * (c + 1))
                if c == 0:
                    pe.wait_ge(s_hf, KT * STEPS)
                    pe.wait_ge(s_v, STEPS)
                else:
                    pe.wait_ge(s_x2, KT * (c - 1) + 1)
                nc.tensor.matmul(bank[6][:], ones[:], ln_acc[:], start=True, stop=True).then_inc(s_l["sum"], 1)

            def ln_var(c):
                pe.wait_ge(s_l["sq_added"], (CT - 1) * (c + 1))
                pe.wait_ge(s_l["mean"], c + 1)
                nc.tensor.matmul(bank[6][:], ones[:], ln_acc[:], start=True, stop=True).then_inc(s_l["var"], 1)

            pe.wait_ge(s_par, 32)
            spread_scale(0)
            pe.wait_ge(s_ones, 48)
            for t in range(STEPS):
                last = t == STEPS - 1
                for f in range(PROJ):
                    project(t, f)
                    if 1 <= f <= F_V:
                        qk_sum(t, f - 1)
                    if f == F_G:
                        transpose_v(t)
                    if f == F_G + 1:
                        qk_spread(t, 0)
                        qk_spread(t, 1)
                        if not last:
                            spread_scale(t + 1)
                    if f == F_G + 2:
                        qk_spread(t, 2)
                        qk_spread(t, 3)
                    if f == F_G + 3:
                        qk_spread(t, 4)
                    if last and f == F_G + 3:
                        ln_sum(0)

            def scores(U):
                c, n, g, ks = unit_of(U)
                rows = slice(HEAD_DIM * g, HEAD_DIM * (g + 1))
                if U % UNITS == 0:
                    pe.wait_ge(s_qkl, 32 * (c + 1))
                if U == 0:
                    for m in range(PROJ * STEPS - SLOTS, PROJ * STEPS):
                        bank_free(m)
                for t in range(GROUP):
                    if U > 0:
                        pe.wait_ge(s_sb, GROUP * (U - 1) + t + 1)
                    nc.tensor.matmul(bank[t][:, P * ks[0]:P * (ks[-1] + 1)], qw[rows, t, P * n:P * (n + 1)],
                                     kw[rows, P * (n + ks[0]):P * (n + ks[-1] + 1)], start=True, stop=True) \
                      .then_inc(s_qk, 1)

            def transposes(U):
                c, n, g, ks = unit_of(U)
                if U == 0:
                    pe.wait_ge(s_qrt, STEPS)
                elif U % UNITS == 0:
                    pe.wait_ge(s_x2, KT * c - 2)
                for kt in ks:
                    i = t_seq[U, kt]
                    if i >= 2:
                        pe.wait_ge(s_pt, i - 1)
                    for t in range(GROUP):
                        pe.wait_ge(s_p, GROUP * U + t + 1)
                        mm = nc.tensor.transpose(bank[4 + i % 2][:, P * t:P * (t + 1)],
                                                 S[U % 2][:, t, P * kt:P * (kt + 1)], ident[:])
                    mm.then_inc(s_t, 1)

            def values(U):
                c, n, g, ks = unit_of(U)
                if U > 0:
                    pe.wait_ge(s_alo, U)
                if U % UNITS == 0:
                    pe.wait_ge(s_vl, 16 * (c + 1))
                    if c > 0:
                        pe.wait_ge(s_x2, KT * c - 1)
                for kt in ks:
                    pe.wait_ge(s_pt, t_seq[U, kt] + 1)
                    mm = nc.tensor.matmul(bank[7][:], vw[:, n + kt, :], PT[U % 2][:, kt, :],
                                          start=(kt == ks[0]), stop=(kt == ks[-1]))
                mm.then_inc(s_pv, 1)

            def norm2_sum(c):
                pe.wait_ge(s_n2a, (KT - 1) * (c + 1))
                if c + 1 < CHUNKS:
                    pe.wait_ge(s_l["log"], c + 2)
                nc.tensor.matmul(bank[6][:], ones[:], n2_acc[:], start=True, stop=True).then_inc(s_n2m, 1)

            def out_half(c, o, attn):
                ks = range(AT) if attn else range(AT, KT)
                if attn:
                    pe.wait_ge(s_alo, UNITS * (c + 1))
                else:
                    pe.wait_ge(s_l["lo"], CT * (c + 1))
                    if c == 0:
                        pe.wait_ge(s_wolo, o + 1)
                    if o == 0 and c > 0:
                        pe.wait_ge(s_n2l, c)
                    if o in (1, 2):
                        pe.wait_ge(s_pt, t_end(UNITS * (c + 1) - 1))
                    if o == 3:
                        pe.wait_ge(s_alo, UNITS * (c + 1))
                    if o >= 4:
                        before = max(i for i in range(o) if OUT_BANKS[i] == OUT_BANKS[o])
                        pe.wait_ge(s_x2, KT * c + before + 1)
                    if o == KT - 1 and c + 1 < CHUNKS:
                        pe.wait_ge(s_l["log"], c + 2)
                for k in ks:
                    for i, (l, r) in enumerate(((wo_hi, cat_hi), (wo_hi, cat_lo), (wo_lo, cat_hi))):
                        mm = nc.tensor.matmul(bank[OUT_BANKS[o]][:], l[:, o, k, :], r[:, k, :],
                                              start=(k == AT and i == 0), stop=(k == AT - 1 and i == 2))
                if attn:
                    mm.then_inc(s_wo, 1)

            scores(0)
            ln_var(0)
            scores(1)
            for c in range(CHUNKS):
                for u in range(UNITS):
                    U = UNITS * c + u
                    transposes(U)
                    if u == 1 and c > 0:
                        norm2_sum(c - 1)
                    if u + 2 < UNITS:
                        scores(U + 2)
                    if u == UNITS - 1:
                        out_half(c, 0, False)
                    values(U)
                if c == CHUNKS - 1:
                    pe.sem_inc(s_used, RING)
                out_half(c, 1, False)
                out_half(c, 0, True)
                out_half(c, 1, True)
                for o in range(1, KT):
                    if o > 1:
                        out_half(c, o, False)
                        if o == 4 and c + 1 < CHUNKS:
                            ln_var(c + 1)
                        out_half(c, o, True)
                    if c + 1 < CHUNKS:
                        if o == 1:
                            ln_sum(c + 1)
                        if o == 2:
                            scores(UNITS * (c + 1))
                        if o == 4:
                            scores(UNITS * (c + 1) + 1)

            passes = ((whi, hw_hi), (whi, hw_lo), (wlo, hw_hi))

            def gate(w, i, s):
                J, base = FT * w + 2 * i + s, TILES_W * w
                pe.wait_ge(s_flo, base + 4 * i + 2 * s + 1 + RING)
                pe.wait_ge(s_gb, J + 1)
                x_ = 0
                for k in range(KT):
                    for l, r in passes:
                        mm = nc.tensor.matmul(bank[s][:, 0:TH], l[2 * s][:, k, :], r[:, k, :],
                                              start=(x_ == 0), stop=(x_ == 3 * KT - 1))
                        x_ += 1
                mm.then_inc(s_used, 1)

            def up(w, i, s):
                J, base = FT * w + 2 * i + s, TILES_W * w
                pe.wait_ge(s_flo, base + 4 * i + 2 * s + 2 + RING)
                pe.wait_ge(s_m, J + 1)
                x_ = 0
                for k in range(KT):
                    for l, r in passes:
                        mm = nc.tensor.matmul(bank[2 + s][:, 0:TC], l[2 * s + 1][:, k, :], r[:, k, 1:TC + 1],
                                              start=(x_ == 0), stop=(x_ == 3 * KT - 1))
                        x_ += 1
                mm.then_inc(s_used, 1)

            for w in range(WINDOWS):
                base = TILES_W * w
                pe.wait_ge(s_hwlo, w + 1)
                if w == 0:
                    for s in range(2):
                        gate(0, 0, s)
                        if s == 0:
                            norm2_sum(CHUNKS - 1)
                        up(0, 0, s)
                with pe.Fori(1 if w == 0 else 0, FT // 2) as i:
                    for s in range(2):
                        gate(w, i, s)
                        up(w, i, s)
                pe.wait_ge(s_mlo, FT * (w + 1))
                for o in range(KT):
                    n = KT * w + o
                    if n >= 2:
                        pe.wait_ge(s_y, n - 1)
                    x_ = 0
                    for s in range(DOWN_PIECES):
                        tile = TILES_F + DOWN_PIECES * o + s
                        slot = tile % RING
                        pe.wait_ge(s_flo, base + tile + 1 + RING)
                        for k in range(W_PIECE * s, min(W_PIECE * (s + 1), FT)):
                            if o == 0 and k >= FT - 2:
                                pe.wait_ge(s_mlo, FT * w + k + 3)
                            for l, r in ((whi, mid_hi(k)), (whi, mid_lo(k)), (wlo, mid_hi(k))):
                                mm = nc.tensor.matmul(bank[4 + o % 2][:, 0:TC], l[slot][:, k - W_PIECE * s, :], r,
                                                      start=(x_ == 0), stop=(x_ == 3 * FT - 1))
                                x_ += 1
                        mm.then_inc(s_used, 1)


def constants():
    ones = np.ones((P, P), np.float32)
    pick = np.zeros((P, 2 * NORM_ROWS - KV_HEADS), np.float32)
    pick[:, NORM_ROWS - KV_HEADS:NORM_ROWS] = np.kron(np.eye(KV_HEADS), np.ones((HEAD_DIM, 1)))
    spread = np.zeros((P, NORMED * P), np.float32)
    spread[:NORM_ROWS] = np.kron(np.eye(NORM_ROWS), np.ones((1, HEAD_DIM)))
    dist = np.abs(np.arange(P)[:, None] + P - np.arange(BAND)[None, :]).astype(np.float32)
    slopes = np.array([2.0 ** (-8.0 * (h + 1) / HEADS) for h in range(HEADS)], np.float32)
    bias = np.where(dist[:, None, :] <= WINDOW, -slopes[None, :, None] * dist[:, None, :], np.float32(NEG))
    return np.concatenate([ones, np.eye(P, dtype=np.float32), pick, spread, bias.reshape(P, -1).astype(np.float32)], 1)


def weight_tiles(w):
    k, n = w.shape
    return w.reshape(k // P, P, n // P, P).transpose(2, 1, 0, 3)


def by_partition(v):
    v = v.reshape(*v.shape[:-1], v.shape[-1] // P, P)
    return np.moveaxis(np.moveaxis(v, -1, 0), -1, 1).reshape(P, -1)


def kernel(**inputs):
    import concourse.bacc as bacc
    from concourse.bass_utils import run_bass_kernel_spmd

    i = {k: np.asarray(v) for k, v in inputs.items()}
    x = np.concatenate([i["x_prompt"][0], i["x_sample"][0]], 0).T.reshape(KT, P, TOKENS).transpose(1, 0, 2)
    w_in = i["w_in"][0]
    q, k, v, glu_a, glu_g = np.split(w_in, [ATTN_W, ATTN_W + KV_W, ATTN_W + 2 * KV_W, ATTN_W + 2 * KV_W + CONV_W], 1)
    q = q.reshape(D_MODEL, KV_HEADS, GROUP, HEAD_DIM).transpose(0, 2, 1, 3).reshape(D_MODEL, ATTN_W)
    glu = np.stack([weight_tiles(glu_a), weight_tiles(glu_g)], 1).reshape(2 * CT, P, KT, P)
    w_in_t = np.concatenate([weight_tiles(k), weight_tiles(q), weight_tiles(v), glu], 0)
    w_out = i["w_out"][0]
    attn_rows = w_out[:ATTN_W].reshape(KV_HEADS, GROUP, HEAD_DIM, D_MODEL).transpose(1, 0, 2, 3)
    w_out_t = weight_tiles(np.concatenate([attn_rows.reshape(ATTN_W, D_MODEL), w_out[ATTN_W:]], 0))
    w_ffn = np.stack([weight_tiles(i["ffn_w_gate"][0]), weight_tiles(i["ffn_w_up"][0])], 1)
    w_ffn = w_ffn.reshape(TILES_F, P, KT, P)
    down = weight_tiles(i["ffn_w_down"][0])
    down = np.concatenate([down, np.zeros((KT, P, DOWN_PIECES * W_PIECE - FT, P), down.dtype)], 2)
    w_down = down.reshape(KT, P, DOWN_PIECES, W_PIECE, P).transpose(0, 2, 1, 3, 4)
    packed = {
        "g1": by_partition(i["norm1_g"][0]), "g2": by_partition(i["norm2_g"][0]),
        "conv_w": by_partition(i["conv_dw_w"][0]),
        "conv_b": by_partition(i["conv_dw_b"][0]),
        "ln_g": by_partition(i["conv_ln_g"][0]), "ln_b": by_partition(i["conv_ln_b"][0]),
        "ffn_w": by_partition(i["ffn_dw_w"][0]),
        "ffn_b": by_partition(i["ffn_dw_b"][0]),
        "q_g": np.tile(i["q_norm_g"][0], 2)[:, None], "k_g": np.tile(i["k_norm_g"][0], 2)[:, None],
        "sink": np.tile(i["attn_sink"][0], (P, 1)),
    }
    params = np.concatenate([packed[name] for name, _ in PARAM_SPLIT], 1)
    x_tok = np.concatenate([i["x_prompt"][0], i["x_sample"][0]], 0).reshape(STEPS, TA // P, P, D_MODEL)
    x_tok = x_tok.transpose(0, 2, 1, 3)
    arrays = {"x_t": x, "x_tok": x_tok, "w_in_t": w_in_t, "w_out_t": w_out_t, "w_ffn_t": w_ffn, "w_down_t": w_down,
              "params": params, "consts": constants()}
    arrays = {name: np.ascontiguousarray(a) for name, a in arrays.items()}

    nc = bacc.Bacc("TRN2", target_bir_lowering=False, num_devices=1)
    args = [nc.dram_tensor(name, a.shape, mybir.dt.from_np(a.dtype), kind="ExternalInput").ap()
            for name, a in arrays.items()]
    y = nc.dram_tensor("y_t", (KT, P, OUT_COLS), F32, kind="ExternalOutput").ap()
    encoder_layer(nc, *args, y)
    got = run_bass_kernel_spmd(nc, [arrays], core_ids=[0]).results[0]["y_t"]
    got = np.asarray(got).reshape(D_MODEL, OUT_COLS).T
    y_prompt = np.ascontiguousarray(got[:PROMPT])[None]
    y_sample = np.ascontiguousarray(got[PROMPT + 1:PROMPT + 1 + SAMPLE])[None]
    return y_prompt, y_sample
```
